# Optimizing a Trainium2 kernel written in Bass

```python
import math, functools
import jax, jax.numpy as jnp
from jax import lax
import numpy as np

D_MODEL = 1024
BATCH = 1
SEQ = 1024
DEPTH = 1
DEC_BATCH = 8
DEC_SEQ = 1
PAST_LEN = 4096
PAGE_SIZE = 128

MLA_HEADS = 8
QK_NOPE = 64
QK_ROPE = 32
QK_DIM = QK_NOPE + QK_ROPE
V_DIM = 64
Q_LORA = 384
KV_LORA = 256
ROPE_THETA = 10000.0
Q_BLOCK = 128
ATTN_SCALE = 1.0 / math.sqrt(QK_DIM)
SSM_HEADS = 8
SSM_HEADDIM = 64
SSM_INNER = SSM_HEADS * SSM_HEADDIM
SSM_GROUPS = 2
D_STATE = 128
CONV_K = 4
CONV_CH = SSM_INNER + 2 * SSM_GROUPS * D_STATE
SSD_CHUNK = 128
MIX_WIDTH = MLA_HEADS * V_DIM + SSM_INNER
IN_SPLITS = [Q_LORA, KV_LORA, QK_ROPE, SSM_INNER, CONV_CH, SSM_HEADS]
IN_COLS = sum(IN_SPLITS)
N_GROUPS = 4
EXPERTS_PER_GROUP = 4
N_EXPERTS = N_GROUPS * EXPERTS_PER_GROUP
EXPERT_FF = 512
TOP_K = 2
PLE_DIM = 256
EPS = 1e-6

kernel_name = "hymba_mla_ssd_hmoe_step"

def rmsnorm(x, g):
    xf = x.astype(jnp.float32)
    xf = xf * lax.rsqrt(jnp.mean(xf * xf, axis=-1, keepdims=True) + EPS)
    return xf.astype(x.dtype) * g

def rope(x, pos):
    half = x.shape[-1] // 2
    inv = ROPE_THETA ** (-jnp.arange(half, dtype=jnp.float32) / half)
    ang = pos.astype(jnp.float32)[:, None] * inv[None, :]
    shape = (1, pos.shape[0]) + (1,) * (x.ndim - 3) + (half,)
    cos = jnp.cos(ang).reshape(shape).astype(x.dtype)
    sin = jnp.sin(ang).reshape(shape).astype(x.dtype)
    x1, x2 = x[..., :half], x[..., half:]
    return jnp.concatenate([x1 * cos - x2 * sin, x1 * sin + x2 * cos], axis=-1)

def mla_prompt_attn(q_nope, q_rope, ckv, krope, w_uk, w_uv):
    B, S, H, _ = q_nope.shape
    k_nope = jnp.einsum('bsc,chd->bshd', ckv, w_uk)
    v = jnp.einsum('bsc,chd->bshd', ckv, w_uv)
    q = jnp.concatenate([q_nope, q_rope], axis=-1)
    k = jnp.concatenate([k_nope, jnp.broadcast_to(krope[:, :, None, :], (B, S, H, QK_ROPE))], axis=-1)
    nb = S // Q_BLOCK
    qb = q.reshape(B, nb, Q_BLOCK, H, QK_DIM).transpose(1, 0, 2, 3, 4)
    kpos = jnp.arange(S)

    def block(args):
        qi, i = args
        s = jnp.einsum('bqhd,bkhd->bhqk', qi, k).astype(jnp.float32) * ATTN_SCALE
        qpos = i * Q_BLOCK + jnp.arange(Q_BLOCK)
        s = jnp.where(kpos[None, :] <= qpos[:, None], s, -jnp.inf)
        p = jax.nn.softmax(s, axis=-1).astype(v.dtype)
        return jnp.einsum('bhqk,bkhd->bqhd', p, v)

    o = lax.map(block, (qb, jnp.arange(nb)))
    return o.transpose(1, 0, 2, 3, 4).reshape(B, S, H, V_DIM)

def mla_paged_attn(q_nope, q_rope, ckv, krope, w_uk, w_uv, cache_ckv, cache_krope, page_table):
    B, L, H, _ = q_nope.shape
    past_ckv = cache_ckv[page_table].reshape(B, -1, KV_LORA)
    past_kr = cache_krope[page_table].reshape(B, -1, QK_ROPE)
    T = past_ckv.shape[1]
    q_lat = jnp.einsum('blhd,chd->blhc', q_nope, w_uk)
    s_past = (jnp.einsum('blhc,btc->bhlt', q_lat, past_ckv)
              + jnp.einsum('blhr,btr->bhlt', q_rope, past_kr)).astype(jnp.float32) * ATTN_SCALE
    s_new = (jnp.einsum('blhc,bsc->bhls', q_lat, ckv)
             + jnp.einsum('blhr,bsr->bhls', q_rope, krope)).astype(jnp.float32) * ATTN_SCALE
    s_new = jnp.where(jnp.tril(jnp.ones((L, L), bool)), s_new, -jnp.inf)
    p = jax.nn.softmax(jnp.concatenate([s_past, s_new], axis=-1), axis=-1).astype(ckv.dtype)
    o_lat = (jnp.einsum('bhlt,btc->blhc', p[..., :T], past_ckv)
             + jnp.einsum('bhls,bsc->blhc', p[..., T:], ckv))
    return jnp.einsum('blhc,chd->blhd', o_lat, w_uv)

def causal_conv(xbc, prev, w, b):
    L = xbc.shape[1]
    xp = jnp.concatenate([prev.astype(xbc.dtype), xbc], axis=1)
    y = sum(xp[:, k:k + L] * w[k] for k in range(CONV_K)) + b
    return y, xp[:, xp.shape[1] - (CONV_K - 1):]

def segsum(a):
    T = a.shape[-1]
    a_rep = jnp.broadcast_to(a[..., None], a.shape + (T,))
    a_rep = jnp.where(jnp.tril(jnp.ones((T, T), bool), -1), a_rep, 0.0)
    s = jnp.cumsum(a_rep, axis=-2)
    return jnp.where(jnp.tril(jnp.ones((T, T), bool)), s, -jnp.inf)

def ssd(x, dt, a, bm, cm, h0, chunk):
    Bsz, L, H, P = x.shape
    N = bm.shape[-1]
    nc = L // chunk
    x = x.astype(jnp.float32).reshape(Bsz, nc, chunk, H, P)
    dt = dt.astype(jnp.float32).reshape(Bsz, nc, chunk, H)
    bm = bm.astype(jnp.float32).reshape(Bsz, nc, chunk, H, N)
    cm = cm.astype(jnp.float32).reshape(Bsz, nc, chunk, H, N)
    dt_h = jnp.moveaxis(dt, -1, 1)
    da = dt_h * a.astype(jnp.float32)[None, :, None, None]
    da_cs = jnp.cumsum(da, axis=-1)
    m = jnp.einsum('bclhn,bcshn->bhcls', cm, bm) * jnp.exp(segsum(da)) * dt_h[:, :, :, None, :]
    y_diag = jnp.einsum('bhcls,bcshp->bclhp', m, x)
    w_end = jnp.exp(da_cs[..., -1:] - da_cs) * dt_h
    states = jnp.einsum('bclhn,bhcl,bclhp->bchpn', bm, w_end, x)
    states = jnp.concatenate([h0.astype(jnp.float32)[:, None], states], axis=1)
    chunk_decay = jnp.exp(segsum(jnp.pad(da_cs[..., -1], ((0, 0), (0, 0), (1, 0)))))
    new_states = jnp.einsum('bhzc,bchpn->bzhpn', chunk_decay, states)
    y_off = jnp.einsum('bclhn,bchpn,bhcl->bclhp', cm, new_states[:, :-1], jnp.exp(da_cs))
    return (y_diag + y_off).reshape(Bsz, L, H, P), new_states[:, -1]

def mixer_block(h, pos, attend, conv_prev, ssm_h0, lw):
    Bsz, L, _ = h.shape
    u = h @ lw['w_in']
    c_q, c_kv, k_r, z, xbc, dt = jnp.split(u, list(np.cumsum(IN_SPLITS[:-1])), axis=-1)
    q = jnp.einsum('blc,chd->blhd', rmsnorm(c_q, lw['norm_q']), lw['w_uq'])
    q_nope, q_rope = q[..., :QK_NOPE], rope(q[..., QK_NOPE:], pos)
    c_kv = rmsnorm(c_kv, lw['norm_kv'])
    k_r = rope(k_r, pos)
    w_uk, w_uv = lw['w_ukv'][..., :QK_NOPE], lw['w_ukv'][..., QK_NOPE:]
    o_attn = attend(q_nope, q_rope, c_kv, k_r, w_uk, w_uv).reshape(Bsz, L, MLA_HEADS * V_DIM)
    o_attn = rmsnorm(o_attn, lw['norm_attn_out'])
    xbc, conv_new = causal_conv(xbc, conv_prev, lw['conv_w'], lw['conv_b'])
    xbc = jax.nn.silu(xbc)
    xs, bm, cm = jnp.split(xbc, [SSM_INNER, SSM_INNER + SSM_GROUPS * D_STATE], axis=-1)
    xs = xs.reshape(Bsz, L, SSM_HEADS, SSM_HEADDIM)
    rep = SSM_HEADS // SSM_GROUPS
    bm = jnp.repeat(bm.reshape(Bsz, L, SSM_GROUPS, D_STATE), rep, axis=2)
    cm = jnp.repeat(cm.reshape(Bsz, L, SSM_GROUPS, D_STATE), rep, axis=2)
    dt = jax.nn.softplus((dt + lw['dt_bias']).astype(jnp.float32))
    a = -jnp.exp(lw['a_log'].astype(jnp.float32))
    chunk = SSD_CHUNK if L % SSD_CHUNK == 0 else L
    y, ssm_new = ssd(xs, dt, a, bm, cm, ssm_h0, chunk)
    y = y.astype(h.dtype) + lw['d_skip'][:, None] * xs
    y = rmsnorm(y.reshape(Bsz, L, SSM_INNER) * jax.nn.silu(z), lw['norm_ssm_out'])
    mix = jnp.concatenate([o_attn, y], axis=-1) @ lw['w_out']
    return mix, (c_kv, k_r, conv_new, ssm_new.astype(h.dtype))

def hier_moe(h, lw):
    T = h.shape[0]
    g_prob = jax.nn.softmax((h @ lw['w_group_router'] + lw['b_group_router']).astype(jnp.float32), axis=-1)
    g_w, g_idx = lax.top_k(g_prob, 1)
    e_logits = (h @ lw['w_expert_router'] + lw['b_expert_router']).astype(jnp.float32)
    e_logits = jnp.take_along_axis(e_logits.reshape(T, N_GROUPS, EXPERTS_PER_GROUP), g_idx[:, :, None], axis=1)[:, 0]
    e_w, e_idx = lax.top_k(jax.nn.softmax(e_logits, axis=-1), TOP_K)
    comb = g_w * (e_w / jnp.sum(e_w, axis=-1, keepdims=True))
    gidx = g_idx * EXPERTS_PER_GROUP + e_idx
    dense = jnp.einsum('tk,tke->te', comb, jax.nn.one_hot(gidx, N_EXPERTS, dtype=jnp.float32)).astype(h.dtype)
    out = jnp.zeros_like(h)
    for e in range(N_EXPERTS):
        act = jax.nn.silu(h @ lw['w_exp_gate'][e]) * (h @ lw['w_exp_up'][e])
        out = out + dense[:, e:e + 1] * (act @ lw['w_exp_down'][e])
    return out

def hybrid_layer(x, p, pos, attend, conv_prev, ssm_h0, lw):
    mix, st = mixer_block(rmsnorm(x, lw['norm_mix']), pos, attend, conv_prev, ssm_h0, lw)
    x = x + mix
    h = rmsnorm(x, lw['norm_ffn'])
    x = x + hier_moe(h.reshape(-1, D_MODEL), lw).reshape(x.shape)
    gate = jax.nn.sigmoid(rmsnorm(x, lw['norm_ple']) @ lw['w_ple_gate'])
    x = x + gate * (p @ lw['w_ple_proj'])
    return x, st

def setup_inputs(seed: int = 0) -> dict:
    key = jax.random.key(seed)
    ks = iter(jax.random.split(key, 48))

    def nrm(shape, scale=1.0):
        return jax.random.normal(next(ks), shape, jnp.float32) * scale

    def gain(shape):
        return 1.0 + nrm(shape, 0.01)

    n_pages = PAST_LEN // PAGE_SIZE
    n_pool = (DEC_BATCH * n_pages * 5) // 4
    page_table = jax.random.permutation(next(ks), n_pool)[:DEC_BATCH * n_pages].reshape(DEC_BATCH, n_pages).astype(jnp.int32)
    dt0 = jnp.exp(jax.random.uniform(next(ks), (DEPTH, SSM_HEADS), jnp.float32, math.log(1e-3), math.log(1e-1)))
    dt_bias = dt0 + jnp.log(-jnp.expm1(-dt0))
    a_log = jnp.log(jax.random.uniform(next(ks), (DEPTH, SSM_HEADS), jnp.float32, 1.0, 16.0))
    return {
        'x_prompt': nrm((BATCH, SEQ, D_MODEL)),
        'x_sample': nrm((DEC_BATCH, DEC_SEQ, D_MODEL)),
        'p_prompt': nrm((DEPTH, BATCH, SEQ, PLE_DIM)),
        'p_sample': nrm((DEPTH, DEC_BATCH, DEC_SEQ, PLE_DIM)),
        'cache_ckv': nrm((DEPTH, n_pool, PAGE_SIZE, KV_LORA)),
        'cache_krope': nrm((DEPTH, n_pool, PAGE_SIZE, QK_ROPE)),
        'state_conv': nrm((DEPTH, DEC_BATCH, CONV_K - 1, CONV_CH)),
        'state_ssm': nrm((DEPTH, DEC_BATCH, SSM_HEADS, SSM_HEADDIM, D_STATE), 0.5),
        'page_table': page_table,
        'norm_mix': gain((DEPTH, D_MODEL)),
        'w_in': nrm((DEPTH, D_MODEL, IN_COLS), D_MODEL ** -0.5),
        'norm_q': gain((DEPTH, Q_LORA)),
        'w_uq': nrm((DEPTH, Q_LORA, MLA_HEADS, QK_DIM), Q_LORA ** -0.5),
        'norm_kv': gain((DEPTH, KV_LORA)),
        'w_ukv': nrm((DEPTH, KV_LORA, MLA_HEADS, QK_NOPE + V_DIM), KV_LORA ** -0.5),
        'norm_attn_out': gain((DEPTH, MLA_HEADS * V_DIM)),
        'conv_w': nrm((DEPTH, CONV_K, CONV_CH), CONV_K ** -0.5),
        'conv_b': nrm((DEPTH, CONV_CH), 0.01),
        'dt_bias': dt_bias,
        'a_log': a_log,
        'd_skip': gain((DEPTH, SSM_HEADS)),
        'norm_ssm_out': gain((DEPTH, SSM_INNER)),
        'w_out': nrm((DEPTH, MIX_WIDTH, D_MODEL), MIX_WIDTH ** -0.5),
        'norm_ffn': gain((DEPTH, D_MODEL)),
        'w_group_router': nrm((DEPTH, D_MODEL, N_GROUPS), D_MODEL ** -0.5),
        'b_group_router': nrm((DEPTH, N_GROUPS), 0.01),
        'w_expert_router': nrm((DEPTH, D_MODEL, N_EXPERTS), D_MODEL ** -0.5),
        'b_expert_router': nrm((DEPTH, N_EXPERTS), 0.01),
        'w_exp_gate': nrm((DEPTH, N_EXPERTS, D_MODEL, EXPERT_FF), D_MODEL ** -0.5),
        'w_exp_up': nrm((DEPTH, N_EXPERTS, D_MODEL, EXPERT_FF), D_MODEL ** -0.5),
        'w_exp_down': nrm((DEPTH, N_EXPERTS, EXPERT_FF, D_MODEL), EXPERT_FF ** -0.5),
        'norm_ple': gain((DEPTH, D_MODEL)),
        'w_ple_gate': nrm((DEPTH, D_MODEL, D_MODEL), D_MODEL ** -0.5),
        'w_ple_proj': nrm((DEPTH, PLE_DIM, D_MODEL), PLE_DIM ** -0.5),
        'norm_final': gain((D_MODEL,)),
    }

def reference(x_prompt, x_sample, p_prompt, p_sample, cache_ckv, cache_krope, state_conv, state_ssm,
              page_table, norm_mix, w_in, norm_q, w_uq, norm_kv, w_ukv, norm_attn_out, conv_w, conv_b,
              dt_bias, a_log, d_skip, norm_ssm_out, w_out, norm_ffn, w_group_router, b_group_router,
              w_expert_router, b_expert_router, w_exp_gate, w_exp_up, w_exp_down, norm_ple, w_ple_gate,
              w_ple_proj, norm_final):
    bp, sp = x_prompt.shape[0], x_prompt.shape[1]
    bs, ls = x_sample.shape[0], x_sample.shape[1]
    pos_p = jnp.arange(sp)
    pos_s = PAST_LEN + jnp.arange(ls)
    conv0 = jnp.zeros((bp, CONV_K - 1, CONV_CH), x_prompt.dtype)
    ssm0 = jnp.zeros((bp, SSM_HEADS, SSM_HEADDIM, D_STATE), x_prompt.dtype)
    xp, xs = x_prompt, x_sample
    st_p_all, st_s_all = [], []
    for i in range(DEPTH):
        lw = dict(w_in=w_in[i], norm_mix=norm_mix[i], norm_q=norm_q[i], w_uq=w_uq[i], norm_kv=norm_kv[i],
                  w_ukv=w_ukv[i], norm_attn_out=norm_attn_out[i], conv_w=conv_w[i], conv_b=conv_b[i],
                  dt_bias=dt_bias[i], a_log=a_log[i], d_skip=d_skip[i], norm_ssm_out=norm_ssm_out[i],
                  w_out=w_out[i], norm_ffn=norm_ffn[i], w_group_router=w_group_router[i],
                  b_group_router=b_group_router[i], w_expert_router=w_expert_router[i],
                  b_expert_router=b_expert_router[i], w_exp_gate=w_exp_gate[i], w_exp_up=w_exp_up[i],
                  w_exp_down=w_exp_down[i], norm_ple=norm_ple[i], w_ple_gate=w_ple_gate[i],
                  w_ple_proj=w_ple_proj[i])
        xp, st_p = hybrid_layer(xp, p_prompt[i], pos_p, mla_prompt_attn, conv0, ssm0, lw)
        attend_s = functools.partial(mla_paged_attn, cache_ckv=cache_ckv[i], cache_krope=cache_krope[i],
                                     page_table=page_table)
        xs, st_s = hybrid_layer(xs, p_sample[i], pos_s, attend_s, state_conv[i], state_ssm[i], lw)
        st_p_all.append(st_p)
        st_s_all.append(st_s)
    ckv_p, kr_p, conv_p, ssm_p = [jnp.stack([s[j] for s in st_p_all]) for j in range(4)]
    ckv_s, kr_s, conv_s, ssm_s = [jnp.stack([s[j] for s in st_s_all]) for j in range(4)]
    y_prompt = rmsnorm(xp, norm_final)
    y_sample = rmsnorm(xs, norm_final)
    return (y_prompt, y_sample, ckv_p, kr_p, conv_p, ssm_p, ckv_s, kr_s, conv_s, ssm_s)


_drawn_inputs = setup_inputs


def setup_inputs(seed=0):
    import zlib

    import numpy as np

    out = dict(_drawn_inputs(seed))
    spreads = {}
    factors = {'norm_mix': 3.394,
     'norm_q': 7.237,
     'norm_kv': 4.198,
     'norm_attn_out': 5.204,
     'conv_b': 3.39,
     'd_skip': 44.004,
     'norm_ssm_out': 5.476,
     'norm_ffn': 4.518,
     'b_group_router': 4.418,
     'b_expert_router': 7.349,
     'norm_ple': 64.0,
     'norm_final': 32.521}
    for name, (base, spread) in spreads.items():
        noise = np.random.default_rng([zlib.crc32(name.encode()), seed]).standard_normal(out[name].shape)
        drawn = base * np.exp(spread * noise) if base else spread * noise
        out[name] = __import__('jax').numpy.asarray(drawn.astype(out[name].dtype))
    for name, factor in factors.items():
        out[name] = (out[name] * factor).astype(out[name].dtype)
    return out
```

```python
from contextlib import ExitStack

import numpy as np
import concourse.bass as bass
from concourse import mybir

ALU = mybir.AluOpType
ACT = mybir.ActivationFunctionType
AX = mybir.AxisListType
F32 = mybir.dt.float32
I32 = mybir.dt.int32
U32 = mybir.dt.uint32

P = 128
D = 1024
KD = D // P
SEQ = 1024
NB = 8
PT = SEQ // P
TILES = PT + 1
ROWS = TILES * P
H = 8
NOPE, ROPE, VD = 64, 32, 64
QD = NOPE + ROPE
QL, KL = 384, 256
CACHE_W = KL + ROPE
PAGES = 32
SCALE = float(QD) ** -0.5
INNER = 512
NST = 128
CT = 8
CK = 4
C_CKV, C_KR, C_Z, C_X, C_DT = QL, QL + KL, QL + KL + ROPE, QL + KL + ROPE + INNER, QL + KL + ROPE + INNER + 1024
IN_COLS = C_DT + H
NE, NG, EPG, FF = 16, 4, 4, 512
KF = FF // P
PLE = 256
EPS = 1e-6
NEG = -1.0e30
PAIRS = 2 * (SEQ + NB)
SLOTS = (PAIRS - NE) // P + NE

BR_GKV, BR_GFIN, BR_DTB, BR_ALOG, BR_DSK, BR_RB = 0, KL, KL + D, KL + D + 8, KL + D + 16, KL + D + 24
BR_W = BR_RB + NG + NE
CO_GMIX, CO_GQ, CO_GOUT, CO_GFFN, CO_GPLE, CO_CW, CO_CB = 0, 8, 11, 19, 27, 35, 35 + CT * CK
CO_W = CO_CB + CT
CS_ID, CS_TRI, CS_CAUS, CS_NEW = 0, P, 2 * P, 3 * P
CS_SLOT = CS_NEW + NB
CS_EYE = CS_SLOT
CS_HSEL = CS_EYE + NB * NB
CS_SEL32 = CS_HSEL + H
CS_NEG = CS_SEL32 + H
CS_IOTA = CS_NEG + 255
CS_REV = CS_IOTA + P
CS_LOW = CS_REV + NE
CS_VALID = CS_LOW + NE * NE
CS_TOK = CS_VALID + 1
CS_W = CS_TOK + TILES


def bc(ap, axis, shape):
    return ap.unsqueeze(axis).broadcast_to(shape)


def later(i):
    return not isinstance(i, int) or i > 0


def program(nc, t_in, t_out):
    x_all, p_t, cache, page_table, conv_prev, ssm_prev = [t_in[n] for n in (
        "x_all", "p_t", "cache", "page_table", "conv_prev", "ssm_prev")]
    w_in, w_uq, w_ukv, w_ukt, w_out, w_rout = [t_in[n] for n in ("w_in", "w_uq", "w_ukv", "w_ukt", "w_out", "w_rout")]

    def scratch(name, shape, dt=F32):
        return nc.dram_tensor(name, shape, dt, kind="Internal").ap()

    qt_d = scratch("qt_d", (QD, H, ROWS))
    kt_d = scratch("kt_d", (QD, H, ROWS))
    v_d = scratch("v_d", (ROWS, H * VD))
    ssm_d = scratch("ssm_d", (ROWS, INNER))
    x2_d = scratch("x2_d", (ROWS, D))
    hn_d = scratch("hn_d", (ROWS, D))
    y_d = scratch("y_d", (SLOTS * P, D))

    with ExitStack() as ctx:
        def sb_in(stack, name, shape, dt=F32):
            return stack.enter_context(nc.sbuf_tensor(name, shape, dt))

        pb = ctx.enter_context(nc.psum_tensor("pb", [P, 8, 512], F32))
        brow = sb_in(ctx, "brow", [P, BR_W])
        cols = sb_in(ctx, "cols", [P, CO_W])
        cst = sb_in(ctx, "cst", [P, CS_W])
        ones = sb_in(ctx, "ones", [P, P])
        arow = sb_in(ctx, "arow", [P, H])
        ident = cst[:, CS_ID:CS_ID + P]
        hsel = cst[:, CS_HSEL:CS_HSEL + H]
        sel32 = cst[:, CS_SEL32:CS_SEL32 + H]
        tri = cst[:, CS_TRI:CS_TRI + P]
        gates = sb_in(ctx, "gates", [P, 2, TILES])
        posg = sb_in(ctx, "posg", [P, 2, TILES], U32)
        tokx = sb_in(ctx, "tokx", [P, SLOTS], U32)
        slot_e = sb_in(ctx, "slot_e", [P, SLOTS], I32)
        mhalf = sb_in(ctx, "mhalf", [P, 2])
        meps = sb_in(ctx, "meps", [P, 2])
        mark = sb_in(ctx, "mark", [P, 1])
        amark = sb_in(ctx, "amark", [P, 1])
        mixer = ExitStack()
        qT = sb_in(mixer, "qT", [QD, H, P])
        qrow = sb_in(mixer, "qrow", [P, H, QD])
        ckvn = sb_in(mixer, "ckvn", [P, KL])
        krn = sb_in(mixer, "krn", [P, ROPE])
        wkv = sb_in(mixer, "wkv", [P, KL // P, H * (NOPE + VD)])

        s = {}

        def S(name):
            if name not in s:
                s[name] = nc.alloc_semaphore(name)
            return s[name]

        def end_phase(*kept):
            nc.clear_and_free_semaphores([x for name, x in s.items() if name not in kept])
            for name in [x for x in s if x not in kept]:
                del s[name]
            nc.all_engine_barrier()

        const_in = S("const_in")

        p1 = ExitStack()
        ssm_rows = sb_in(p1, "ssm_rows", [P, TILES, INNER])
        w1 = sb_in(p1, "w1", [P, KD, IN_COLS])
        wq = sb_in(p1, "wq", [P, QL // P, H * QD])
        cs16 = sb_in(p1, "cs16", [P, TILES, ROPE])
        xt = sb_in(p1, "xt", [P, D])
        xn = sb_in(p1, "xn", [P, D])
        hT = sb_in(p1, "hT", [P, KD, P])
        cqn = sb_in(p1, "cqn", [P, QL])
        sq = sb_in(p1, "sq", [P, 512])
        stat = sb_in(p1, "stat", [P, 16])
        krow = sb_in(p1, "krow", [P, H, QD])
        rt = sb_in(p1, "rt", [P, 4, 4, 16])
        rk = sb_in(p1, "rk", [P, 4, 16])
        cT = sb_in(p1, "cT", [P, 5, P])
        vrow = sb_in(p1, "vrow", [P, H, VD])
        kT = sb_in(p1, "kT", [QD, H, P])
        zs = sb_in(p1, "zs", [P, INNER])
        xraw = sb_in(p1, "xraw", [P, CT, CK - 1 + P])
        conv = sb_in(p1, "conv", [P, CT, P])
        xbcT = sb_in(p1, "xbcT", [P, CT, P])
        xrow = sb_in(p1, "xrow", [P, INNER])
        brw = sb_in(p1, "brw", [P, 2 * NST])
        dtr = sb_in(p1, "dtr", [P, H])
        dtw = sb_in(p1, "dtw", [P, 12, H])
        dt = sb_in(p1, "dt", [P, H])
        da = sb_in(p1, "da", [P, H])
        cd = sb_in(p1, "cd", [P, 3, H])
        ew = sb_in(p1, "ew", [P, 3, H])
        wend = sb_in(p1, "wend", [P, H])
        gm = sb_in(p1, "gm", [P, 2, P])
        dd = sb_in(p1, "dd", [P, H, P])
        mT = sb_in(p1, "mT", [P, H, P])
        xw = sb_in(p1, "xw", [P, INNER])
        state = sb_in(p1, "state", [P, INNER])
        st1 = sb_in(p1, "st1", [P, INNER])
        yb = sb_in(p1, "yb", [P, 5, INNER])

        lastraw = sb_in(p1, "lastraw", [P, CT, CK - 1])
        cprev = sb_in(p1, "cprev", [P, CT, CK - 1, NB])
        cnew = sb_in(p1, "cnew", [P, CT, CK - 1, NB])
        cconv = sb_in(p1, "cconv", [P, CT, NB])
        w1f = w1[:, :, :].rearrange("p k n -> p (k n)")
        shist = w1f[:, 0:4096]
        snew = w1f[:, 4096:8192]
        sdec = sb_in(p1, "sdec", [P, NB * H])
        xdt = sb_in(p1, "xdt", [P, INNER])
        sx = w1f[:, 8192:8192 + 4096].rearrange("p (b n) -> p b n", b=NB)
        decm = sb_in(p1, "decm", [P, NB, H])
        cm = sb_in(p1, "cm", [P, 2, NB, NB])
        t_eye = cst[:, CS_EYE:CS_EYE + NB * NB].rearrange("p (b c) -> p b c", b=NB)

        w1_in, cs_in, x_in = S("w1_in"), S("cs_in"), S("x_in")

        def decode_io(sp):
            sp.wait_ge(S("kv_mm"), 2 * TILES)
            sp.dma_start(shist, ssm_prev).then_inc(S("shist_in"), 16)
            sp.wait_ge(S("cnew_rdy"), 2)
            sp.dma_start(t_out["conv_s"], cnew[:, :, :, :]).then_inc(S("tail_st"), 16)
            sp.wait_ge(S("snew_rdy"), NB)
            sp.dma_start(t_out["ssm_s"], snew).then_inc(S("tail_st"), 16)
            sp.wait_ge(S("y_out"), TILES)
            sp.dma_start(ssm_d[SEQ:, :], ssm_rows[:, PT, :]).then_inc(S("ssm_st"), 16)
            sp.wait_ge(S("tail_st"), 64)
            sp.wait_ge(S("ssm_st"), 32)

        block = nc.Block()
        block.__enter__()

        @block.sync
        def _(sp):
            sp.dma_start(brow[:, :], t_in["brow"]).then_inc(const_in, 16)
            sp.dma_start(cols[:, :], t_in["cols"]).then_inc(const_in, 16)
            sp.dma_start(cst[:, :], t_in["cst"]).then_inc(const_in, 16)

            def load_x(i):
                sp.dma_start(xt[:, :], x_all[bass.ds(i * P, P), :]).then_inc(x_in, 16)

            load_x(0)
            sp.dma_start(cs16[:, :, :], t_in["rope"].rearrange("(t p) n -> p t n", p=P)).then_inc(cs_in, 16)
            wv = w_in.rearrange("(k p) n -> p k n", p=P)
            for a, b in ((0, C_CKV), (C_CKV, C_Z), (C_DT, IN_COLS), (C_Z, C_X), (C_X, C_DT)):
                sp.dma_start(w1[:, :, a:b], wv[:, :, a:b]).then_inc(S(f"w1_{a}"), 16)
            sp.dma_start(wq[:, :, :], w_uq.rearrange("(k p) n -> p k n", p=P)).then_inc(w1_in, 16)
            sp.dma_start(wkv[:, :, :], w_ukv.rearrange("(k p) n -> p k n", p=P)).then_inc(w1_in, 16)
            sp.dma_start(cprev[:, :, :, :], conv_prev).then_inc(S("cprev_in"), 16)
            sp.wait_ge(S("xn_rdy"), 1)
            load_x(1)

            def store_rows(i):
                sp.wait_ge(S("ckvn_rdy"), i + 1)
                sp.dma_start(t_out["ckv"][bass.ds(i * P, P), :], ckvn[:, :]).then_inc(S("ckv_st"), 16)
                sp.wait_ge(S("krn_rdy"), i + 1)
                sp.dma_start(t_out["krope"][bass.ds(i * P, P), :], krn[:, :]).then_inc(S("kr_st"), 16)
                sp.wait_ge(S("v_rdy"), 2 * i + 2)
                sp.dma_start(v_d[bass.ds(i * P, P), :], vrow[:, :, :].rearrange("p h d -> p (h d)")).then_inc(S("v_st"), 16)

            def store_heads(j):
                sp.wait_ge(S("qT_rdy"), 2 * j + 2)
                sp.dma_start(qt_d[:, :, bass.ds(j * P, P)], qT[:, :, :]).then_inc(S("q_st"), 16)
                sp.wait_ge(S("kT_rdy"), 2 * j + 2)
                sp.dma_start(kt_d[:, :, bass.ds(j * P, P)], kT[:, :, :]).then_inc(S("k_st"), 16)

            store_rows(0)
            with sp.Fori(1, TILES) as i:
                sp.wait_ge(S("xn_rdy"), i + 1)
                load_x(i + 1)
                store_heads(i - 1)
                store_rows(i)
            sp.wait_ge(S("last_raw"), 1)
            sp.dma_start(t_out["conv_p"], lastraw[:, :, :]).then_inc(S("tail_st"), 16)
            sp.wait_ge(S("state_rdy"), PT)
            sp.dma_start(t_out["ssm_p"], state[:, :]).then_inc(S("tail_st"), 16)
            sp.wait_ge(S("y_out"), PT)
            sp.dma_start(ssm_d[0:SEQ, :].rearrange("(t p) n -> p t n", p=P), ssm_rows[:, 0:PT, :]).then_inc(S("ssm_st"), 16)
            sp.wait_ge(x_in, 16 * (TILES + 1))
            for name in ("ckv_st", "kr_st", "v_st"):
                sp.wait_ge(S(name), 16 * TILES)
            for name in ("q_st", "k_st"):
                sp.wait_ge(S(name), 16 * PT)
            decode_io(sp)

        T = [pb[:, 0, :], pb[:, 1, :]]

        def pe_turn_x(pe, i):
            pe.wait_ge(S("xn_rdy"), i + 1)
            for half in range(2):
                if later(i):
                    pe.wait_ge(S("cT_rdy"), 2 * i)
                for k in range(4):
                    last = pe.transpose(T[half][:, k * P:(k + 1) * P], xn[:, (4 * half + k) * P:(4 * half + k + 1) * P], ident)
                last.then_inc(S("xT_tr"), 1)

        def pe_project(pe, i):
            first = isinstance(i, int)
            pe.wait_ge(S("hT_rdy"), 2 * i + 2)

            def rows(bank, at, a, b):
                for k in range(KD):
                    last = pe.matmul(pb[:, bank, at:at + b - a], hT[:, k, :], w1[:, k, a:b], start=k == 0, stop=k == KD - 1)
                return last
            def arrived(*columns):
                if first:
                    for a in columns:
                        pe.wait_ge(S(f"w1_{a}"), 16)
            arrived(0, C_CKV, C_DT)
            if not first:
                pe.wait_ge(S("q_rope"), 2 * i)
                pe.wait_ge(S("q_nope"), 2 * i)
                pe.wait_ge(S("yo_used"), i - 1)
                pe.wait_ge(S("state_rdy"), i - 1)
            rows(2, 0, 0, C_CKV).then_inc(S("cq_mm"), 1)
            rows(3, 0, C_CKV, C_Z)
            rows(3, C_Z - C_CKV, C_DT, IN_COLS).then_inc(S("ckv_mm"), 1)
            if not first:
                pe.wait_ge(S("zs_rdy"), i)
            arrived(C_Z, C_X)
            rows(4, 0, C_Z, C_X).then_inc(S("z_mm"), 1)
            if not first:
                pe.wait_ge(S("v_rdy"), 2 * i)
                pe.wait_ge(S("k_nope"), 2 * i)
            for c in range(CT):
                for k in range(KD):
                    a = C_X + c * P
                    last = pe.matmul(pb[:, 5 + c // 4, c % 4 * P:(c % 4 + 1) * P], w1[:, k, a:a + P], hT[:, k, :],
                                     start=k == 0, stop=k == KD - 1)
                if c % 4 == 3:
                    last.then_inc(S("xbc_mm"), 1)

        def pe_turn_c(pe, i):
            pe.wait_ge(S("cqn_rdy"), i + 1)
            if isinstance(i, int):
                pe.wait_ge(S("hT_rdy"), 2)
            else:
                pe.wait_ge(S("kT_rdy"), 2 * i)
            for k in range(QL // P):
                last = pe.transpose(T[0][:, k * P:(k + 1) * P], cqn[:, k * P:(k + 1) * P], ident)
            last.then_inc(S("c_tr"), 1)
            pe.wait_ge(S("ckvn_rdy"), i + 1)
            for k in range(KL // P):
                last = pe.transpose(T[1][:, k * P:(k + 1) * P], ckvn[:, k * P:(k + 1) * P], ident)
            last.then_inc(S("c_tr"), 1)

        def pe_heads(pe, i):
            if isinstance(i, int):
                pe.wait_ge(w1_in, 32)
            pe.wait_ge(S("cT_rdy"), 2 * i + 1)
            if isinstance(i, int):
                pe.wait_ge(S("cqn_rdy"), 1)
                pe.wait_ge(S("dtr_rdy"), 1)
            else:
                pe.wait_ge(S("dd_rdy"), i)
            for half in range(2):
                for k in range(QL // P):
                    last = pe.matmul(pb[:, 2 + half, 0:4 * QD], cT[:, k, :], wq[:, k, half * 4 * QD:(half + 1) * 4 * QD],
                                     start=k == 0, stop=k == QL // P - 1)
                last.then_inc(S("q_mm"), 1)
            pe.wait_ge(S("cT_rdy"), 2 * i + 2)
            pe.wait_ge(S("xraw_rdy"), 2 * i + 2)
            for half in range(2):
                for k in range(KL // P):
                    last = pe.matmul(pb[:, 5 + half, :], cT[:, 3 + k, :], wkv[:, k, half * 512:(half + 1) * 512],
                                     start=k == 0, stop=k == KL // P - 1)
                last.then_inc(S("kv_mm"), 1)

        def pe_turn_heads(pe, j):
            pe.wait_ge(S("q_nope"), 2 * j + 2)
            pe.wait_ge(S("q_rope"), 2 * j + 2)
            pe.wait_ge(S("k_nope"), 2 * j + 2)
            pe.wait_ge(S("k_rope"), j + 1)
            for half in range(2):
                pe.wait_ge(S("xr_rdy"), 2 * j + 1 + half)
                for h in range(4):
                    last = pe.transpose(T[half][0:QD, h * P:(h + 1) * P], qrow[:, 4 * half + h, :], ident)
                last.then_inc(S("q_tr"), 1)
            if isinstance(j, int):
                return
            for half in range(2):
                pe.wait_ge(S("qT_rdy"), 2 * j + 1 + half)
                for h in range(4):
                    last = pe.transpose(T[half][0:QD, h * P:(h + 1) * P], krow[:, 4 * half + h, :], ident)
                last.then_inc(S("k_tr"), 1)

        def pe_turn_channels(pe, j):
            pe.wait_ge(S("xbcT_rdy"), j + 1)
            pe.wait_ge(S("hT_rdy"), 2 * j + 4 if not isinstance(j, int) else 2 * TILES)
            if isinstance(j, int):
                pe.wait_ge(S("cT_rdy"), 2 * TILES)
            for c in range(4):
                last = pe.transpose(T[0][:, c * P:(c + 1) * P], xbcT[:, c, :], ident)
            last.then_inc(S("xr_tr"), 1)
            for c in range(2):
                last = pe.transpose(T[1][:, c * P:(c + 1) * P], xbcT[:, 4 + c, :], ident)
            last.then_inc(S("xr_tr"), 1)

        def pe_chunk_a(pe, j):
            pe_turn_channels(pe, j)
            pe.wait_ge(S("da_rdy"), j + 1)
            pe.wait_ge(S("y_diag_used"), j)
            pe.matmul(pb[:, 7, 0:H], tri, da[:, :], start=True, stop=True)
            pe.matmul(pb[:, 7, H:2 * H], ones[:, :], da[:, :], start=True, stop=True)
            for g in range(2):
                last = pe.matmul(pb[:, 7, P + g * P:P + (g + 1) * P], xbcT[:, 4 + g, :], xbcT[:, 6 + g, :], start=True, stop=True)
            last.then_inc(S("g_mm"), 1)
            pe.wait_ge(S("cqn_rdy"), j + 2)
            pe.wait_ge(S("ckvn_rdy"), j + 2)
            pe.wait_ge(S("krn_rdy"), j + 2)
            pe.wait_ge(S("dtr_rdy"), j + 2)
            for h in range(H):
                last = pe.matmul(pb[:, 2 + h // 4, h % 4 * P:(h % 4 + 1) * P], da[:, h:h + 1].broadcast_to([P, P]), tri,
                                 start=True, stop=True)
                if h % 4 == 3:
                    last.then_inc(S("csb_mm"), 1)

        def pe_chunk_b(pe, j):
            pe.wait_ge(S("mT_rdy"), j + 1)
            pe.wait_ge(S("xr_rdy"), 2 * j + 2)
            for h in range(H):
                last = pe.matmul(pb[:, 7, h * 64:(h + 1) * 64], mT[:, h, :], xrow[:, h * 64:(h + 1) * 64], start=True, stop=True)
            last.then_inc(S("yd_mm"), 1)
            pe.wait_ge(S("q_rope"), 2 * j + 4)
            pe.wait_ge(S("q_nope"), 2 * j + 4)
            pe.wait_ge(S("state_rdy"), j)
            for g in range(2):
                last = pe.matmul(pb[:, 2, g * 256:(g + 1) * 256], xbcT[:, 6 + g, :], state[:, g * 256:(g + 1) * 256],
                                 start=True, stop=True)
            last.then_inc(S("yo_mm"), 1)
            pe.wait_ge(S("xw_rdy"), j + 1)
            for g in range(2):
                last = pe.matmul(pb[:, 3, g * 256:(g + 1) * 256], brw[:, g * P:(g + 1) * P], xw[:, g * 256:(g + 1) * 256],
                                 start=True, stop=True)
            last.then_inc(S("st_mm"), 1)

        def pe_decode(pe):
            j = TILES - 1
            pe_turn_channels(pe, j)
            pe_turn_heads(pe, j)
            pe.wait_ge(S("decm_rdy"), 1)
            pe.wait_ge(S("y_diag_used"), PT)
            pe.matmul(pb[:, 7, 0:NB * H], ones[:, :], decm[:, :, :].rearrange("p b h -> p (b h)"), start=True, stop=True).then_inc(S("sdec_mm"), 1)
            pe.wait_ge(S("cm_rdy"), 1)
            pe.wait_ge(S("state_rdy"), PT)
            pe.wait_ge(S("yo_used"), PT)
            for b in range(NB):
                pe.wait_ge(S("sx_rdy"), b + 1)
                if b > 1:
                    pe.wait_ge(S("snew_rdy"), b - 1)
                for g in range(2):
                    last = pe.matmul(pb[:, 2 + b % 2, g * 256:(g + 1) * 256], brw[:, g * P:(g + 1) * P],
                                     sx[:, b, g * 256:(g + 1) * 256], start=True, stop=True)
                last.then_inc(S("bx_mm"), 1)
            pe.wait_ge(S("v_rdy"), 2 * TILES)
            pe.wait_ge(S("k_nope"), 2 * TILES)
            for g in range(2):
                for b in range(NB):
                    pe.wait_ge(S("snew_rdy"), b + 1)
                    last = pe.matmul(pb[0:NB, 5 + g, 0:256], cm[:, g, b, :], snew[:, b * 512 + g * 256:b * 512 + (g + 1) * 256],
                                     start=b == 0, stop=b == NB - 1)
            last.then_inc(S("ys_mm"), 1)

        @block.tensor
        def _(pe):
            pe.wait_ge(const_in, 3 * 16)
            pe_turn_x(pe, 0)
            pe_project(pe, 0)
            pe_turn_c(pe, 0)
            pe_heads(pe, 0)
            pe.wait_ge(S("ones_rdy"), 4)
            with pe.Fori(1, TILES) as i:
                pe_turn_x(pe, i)
                pe_project(pe, i)
                pe_chunk_a(pe, i - 1)
                pe_turn_heads(pe, i - 1)
                pe_turn_c(pe, i)
                pe_heads(pe, i)
                pe_chunk_b(pe, i - 1)
            pe_decode(pe)

        @block.gpsimd
        def _(pool):
            pool.memset(ones[:, :], 1.0).then_inc(S("ones_rdy"), 1)
            pool.memset(mhalf[:, :], -0.5).then_inc(S("ones_rdy"), 1)
            pool.memset(meps[:, :], EPS).then_inc(S("ones_rdy"), 1)
            pool.memset(state[:, :], 0.0).then_inc(S("ones_rdy"), 1)
            pool.wait_ge(S("ones_rdy"), 4)

            def x_norm(i):
                pool.wait_ge(S("x_sq"), i + 1)
                if later(i):
                    pool.wait_ge(S("xn_rdy"), i)
                pool.tensor_tensor(stat[:, 1:2], stat[:, 0:1], meps[:, 0:1], ALU.add).then_inc(S("x_var"), 1)
                pool.wait_ge(S("x_var"), i + 1)
                pool.tensor_tensor(stat[:, 2:3], stat[:, 1:2], mhalf[:, 0:1], ALU.pow).then_inc(S("x_rs"), 1)

            def c_norm(i):
                pool.wait_ge(S("c_sq"), 2 * i + 2)
                if later(i):
                    pool.wait_ge(S("cqn_rdy"), i)
                    pool.wait_ge(S("ckvn_rdy"), i)
                pool.tensor_tensor(stat[:, 5:7], stat[:, 3:5], meps[:, 0:2], ALU.add).then_inc(S("c_var"), 1)
                pool.wait_ge(S("c_var"), i + 1)
                pool.tensor_tensor(stat[:, 7:9], stat[:, 5:7], mhalf[:, 0:2], ALU.pow).then_inc(S("c_rs"), 1)

            def y_norm(j):
                pool.wait_ge(S("y_sq"), j + 1)
                if later(j):
                    pool.wait_ge(S("y_out"), j)
                pool.tensor_tensor(stat[:, 10:11], stat[:, 9:10], meps[:, 0:1], ALU.add).then_inc(S("y_var"), 1)
                pool.wait_ge(S("y_var"), j + 1)
                pool.tensor_tensor(stat[:, 11:12], stat[:, 10:11], mhalf[:, 0:1], ALU.pow).then_inc(S("y_rs"), 1)

            x_norm(0)
            c_norm(0)
            x_norm(1)
            with pool.Fori(1, TILES) as i:
                c_norm(i)
                x_norm(i + 1)
                y_norm(i - 1)
            y_norm(TILES - 1)

        def act_x(act, i):
            act.wait_ge(x_in, 16 * i + 16)
            if later(i):
                act.wait_ge(S("xT_tr"), 2 * i)
                act.wait_ge(S("x_rs"), i)
            act.activation(xn[:, :], xt[:, :], ACT.Square, scale=D ** -0.5, accum_out=stat[:, 0:1]).then_inc(S("x_sq"), 1)
            act.wait_ge(S("x_rs"), i + 1)
            act.activation(xn[:, :], xt[:, :], ACT.Copy, scale=stat[:, 2:3]).then_inc(S("xn_rdy"), 1)

        def act_latents(act, i):
            act.wait_ge(S("cq_mm"), i + 1)
            if later(i):
                act.wait_ge(S("c_rs"), i)
                act.wait_ge(S("c_tr"), 2 * i)
                act.wait_ge(S("y_sq"), i - 1)
            act.activation(sq[:, 0:QL], pb[:, 2, 0:QL], ACT.Square, scale=QL ** -0.5, accum_out=stat[:, 3:4]).then_inc(S("c_sq"), 1)
            act.wait_ge(S("ckv_mm"), i + 1)
            act.wait_ge(S("c_sq"), 2 * i + 1)
            act.activation(sq[:, 0:KL], pb[:, 3, 0:KL], ACT.Square, scale=KL ** -0.5, accum_out=stat[:, 4:5]).then_inc(S("c_sq"), 1)
            act.wait_ge(S("c_rs"), i + 1)
            act.activation(cqn[:, :], pb[:, 2, 0:QL], ACT.Copy, scale=stat[:, 7:8]).then_inc(S("cqn_rdy"), 1)

        def act_raw(act, i):
            if not isinstance(i, int):
                act.wait_ge(S("hist_rdy"), i + 1)
            else:
                act.wait_ge(S("hist_rdy"), 1)
            for half in range(2):
                act.wait_ge(S("xbc_mm"), 2 * i + 1 + half)
                act.copy(xraw[:, 4 * half:4 * half + 4, CK - 1:], pb[:, 5 + half, :].rearrange("p (c t) -> p c t", c=4)).then_inc(S("xraw_rdy"), 1)

        def act_heads(act, i):
            if later(i):
                act.wait_ge(S("q_tr"), 2 * i)
                act.wait_ge(S("k_tr"), 2 * i)
                act.wait_ge(S("v_st"), 16 * i)
            for half in range(2):
                act.wait_ge(S("q_mm"), 2 * i + 1 + half)
                act.copy(qrow[:, 4 * half:4 * half + 4, 0:NOPE],
                         pb[:, 2 + half, 0:4 * QD].rearrange("p (h d) -> p h d", h=4)[:, :, 0:NOPE]).then_inc(S("q_nope"), 1)
            for half in range(2):
                kv = pb[:, 5 + half, :].rearrange("p (h d) -> p h d", h=4)
                act.wait_ge(S("kv_mm"), 2 * i + 1 + half)
                act.copy(krow[:, 4 * half:4 * half + 4, 0:NOPE], kv[:, :, 0:NOPE]).then_inc(S("k_nope"), 1)
                act.copy(vrow[:, 4 * half:4 * half + 4, :], kv[:, :, NOPE:]).then_inc(S("v_rdy"), 1)

        def act_z(act, i):
            act.wait_ge(S("z_mm"), i + 1)
            if later(i):
                act.wait_ge(S("y_rdy"), i)
            act.activation(zs[:, :], pb[:, 4, :], ACT.Silu).then_inc(S("zs_rdy"), 1)

        def act_silu_dt(act, j):
            act.wait_ge(S("conv_rdy"), j + 1)
            act.wait_ge(S("st_mm"), j)
            act.activation(xbcT[:, :, :], conv[:, :, :], ACT.Silu).then_inc(S("xbcT_rdy"), 1)
            act.wait_ge(S("dt_neg"), j + 1)
            act.wait_ge(S("dt_rdy"), j)
            act.activation(dtw[:, 2, :], dtw[:, 1, :], ACT.Exp).then_inc(S("dt_exp"), 1)
            act.wait_ge(S("dt_one"), j + 1)
            act.activation(dtw[:, 6, :], dtw[:, 3, :], ACT.Ln).then_inc(S("dt_ln"), 1)

        def act_rows(act, j):
            act.wait_ge(S("xr_tr"), 2 * j + 1)
            act.wait_ge(S("y_rdy"), j)
            act.wait_ge(S("st_mm"), j)
            act.copy(xrow[:, :], T[0]).then_inc(S("xr_rdy"), 1)
            act.wait_ge(S("xr_tr"), 2 * j + 2)
            act.copy(brw[:, :], T[1][:, 0:2 * NST]).then_inc(S("xr_rdy"), 1)

        def act_turned(act, j):
            if later(j):
                act.wait_ge(S("q_st"), 16 * j)
            for half in range(2):
                act.wait_ge(S("q_tr"), 2 * j + 1 + half)
                act.copy(qT[:, 4 * half:4 * half + 4, :], T[half][0:QD, :].rearrange("p (h t) -> p h t", h=4)).then_inc(S("qT_rdy"), 1)

        def act_y(act, j):
            act.wait_ge(S("y_rdy"), j + 1)
            act.wait_ge(S("c_sq"), 2 * j + 4 if not isinstance(j, int) else 2 * TILES)
            act.wait_ge(S("y_rs"), j)
            act.activation(sq[:, :], yb[:, 4, :], ACT.Square, scale=INNER ** -0.5, accum_out=stat[:, 9:10]).then_inc(S("y_sq"), 1)
            act.wait_ge(S("y_rs"), j + 1)
            act.activation(ssm_rows[:, j, :], yb[:, 4, :], ACT.Copy, scale=stat[:, 11:12]).then_inc(S("y_out"), 1)

        @block.scalar
        def _(act):
            act.wait_ge(const_in, 3 * 16)
            act.activation(arow[:, :], brow[:, BR_ALOG:BR_ALOG + H], ACT.Exp).then_inc(S("a_exp"), 1)
            act_x(act, 0)
            act_latents(act, 0)
            act_x(act, 1)
            act_raw(act, 0)
            act_heads(act, 0)
            act_z(act, 0)
            with act.Fori(1, TILES) as i:
                j = i - 1
                act_silu_dt(act, j)
                act_latents(act, i)
                act_x(act, i + 1)
                act_rows(act, j)
                act.wait_ge(S("cd_rdy"), i)
                act.activation(ew[:, :, :], cd[:, :, :], ACT.Exp).then_inc(S("ew_rdy"), 1)
                act.wait_ge(S("dd_rdy"), i)
                act.activation(mT[:, :, :], dd[:, :, :], ACT.Exp).then_inc(S("dexp_rdy"), 1)
                act_turned(act, j)
                act_raw(act, i)
                act_heads(act, i)
                act_y(act, j)
                act_z(act, i)
            j = TILES - 1
            act.wait_ge(S("conv_rdy"), TILES)
            act.wait_ge(S("st_mm"), PT)
            act.activation(xbcT[:, :, :], conv[:, :, :], ACT.Silu).then_inc(S("xbcT_rdy"), 1)
            act.wait_ge(S("dt_neg"), TILES)
            act.activation(dtw[:, 2, :], dtw[:, 1, :], ACT.Exp).then_inc(S("dt_exp"), 1)
            act.wait_ge(S("dt_one"), TILES)
            act.activation(dtw[:, 6, :], dtw[:, 3, :], ACT.Ln).then_inc(S("dt_ln"), 1)
            act.wait_ge(S("da_rdy"), TILES)
            act.wait_ge(S("state_rdy"), PT)
            act.wait_ge(S("y_rdy"), PT)
            act.activation(ew[:, 0, :], da[:, :], ACT.Exp).then_inc(S("ew_rdy"), 1)
            act_rows(act, j)
            act_turned(act, j)
            act_y(act, j)

        def dve_turned_x(dve, i):
            for half in range(2):
                dve.wait_ge(S("xT_tr"), 2 * i + 1 + half)
                if half == 0 and not (isinstance(i, int) and i == 0):
                    dve.wait_ge(S("xbc_mm"), 2 * i)
                dve.tensor_tensor(hT[:, 4 * half:4 * half + 4, :], T[half].rearrange("p (k t) -> p k t", k=4),
                                  bc(cols[:, CO_GMIX + 4 * half:CO_GMIX + 4 * half + 4], 2, [P, 4, P]), ALU.mult).then_inc(S("hT_rdy"), 1)

        def rope_terms(dve, x1, x2, cos, sin, n):
            for m, (x, f) in enumerate(((x1, cos), (x2, sin), (x1, sin), (x2, cos))):
                last = dve.tensor_tensor(rt[:, m, 0:n, :], x, f, ALU.mult)
            return last

        def dve_latents(dve, i):
            cos, sin = cs16[:, i, 0:16], cs16[:, i, 16:32]
            dve.wait_ge(S("ckv_mm"), i + 1)
            if later(i):
                dve.wait_ge(S("kr_st"), 16 * i)
                dve.wait_ge(S("ckv_st"), 16 * i)
                dve.wait_ge(S("c_tr"), 2 * i)
                dve.wait_ge(S("q_rope"), 2 * i)
                dve.wait_ge(S("k_rope"), i)
            dve.wait_ge(S("c_sq"), 2 * i + 2)
            kr = pb[:, 3, KL:KL + ROPE]
            rope_terms(dve, kr[:, 0:16].unsqueeze(1), kr[:, 16:32].unsqueeze(1), cos.unsqueeze(1), sin.unsqueeze(1), 1).then_inc(S("kr_terms"), 1)
            dve.tensor_copy(dtr[:, :], pb[:, 3, CACHE_W:CACHE_W + H]).then_inc(S("dtr_rdy"), 1)
            dve.wait_ge(S("kr_terms"), i + 1)
            dve.tensor_tensor(krn[:, 0:16], rt[:, 0, 0, :], rt[:, 1, 0, :], ALU.subtract)
            dve.tensor_tensor(krn[:, 16:32], rt[:, 2, 0, :], rt[:, 3, 0, :], ALU.add).then_inc(S("krn_rdy"), 1)
            dve.wait_ge(S("c_rs"), i + 1)
            dve.scalar_tensor_tensor(ckvn[:, :], pb[:, 3, 0:KL], stat[:, 8:9], brow[:, BR_GKV:BR_GKV + KL],
                                     ALU.mult, ALU.mult).then_inc(S("ckvn_rdy"), 1)

        def dve_turned_c(dve, i):
            dve.wait_ge(S("c_tr"), 2 * i + 1)
            if later(i):
                dve.wait_ge(S("kv_mm"), 2 * i)
            dve.tensor_tensor(cT[:, 0:3, :], T[0][:, 0:3 * P].rearrange("p (k t) -> p k t", k=3),
                              bc(cols[:, CO_GQ:CO_GQ + 3], 2, [P, 3, P]), ALU.mult).then_inc(S("cT_rdy"), 1)
            dve.wait_ge(S("c_tr"), 2 * i + 2)
            dve.tensor_copy(cT[:, 3:5, :], T[1][:, 0:2 * P].rearrange("p (k t) -> p k t", k=2)).then_inc(S("cT_rdy"), 1)

        def dve_rope_heads(dve, i):
            cos, sin = bc(cs16[:, i, 0:16], 1, [P, 4, 16]), bc(cs16[:, i, 16:32], 1, [P, 4, 16])
            if later(i):
                dve.wait_ge(S("k_tr"), 2 * i)
                dve.wait_ge(S("q_tr"), 2 * i)
            dve.wait_ge(S("krn_rdy"), i + 1)
            dve.tensor_copy(krow[:, :, NOPE:], bc(krn[:, :], 1, [P, H, ROPE])).then_inc(S("k_rope"), 1)
            for half in range(2):
                q = pb[:, 2 + half, 0:4 * QD].rearrange("p (h d) -> p h d", h=4)
                dve.wait_ge(S("q_nope"), 2 * i + 1 + half)
                if half:
                    dve.wait_ge(S("q_rope"), 2 * i + 1)
                rope_terms(dve, q[:, :, NOPE:NOPE + 16], q[:, :, NOPE + 16:QD], cos, sin, 4).then_inc(S("q_terms"), 1)
                dve.wait_ge(S("q_terms"), 2 * i + 1 + half)
                dve.tensor_tensor(qrow[:, 4 * half:4 * half + 4, NOPE:NOPE + 16], rt[:, 0, :, :], rt[:, 1, :, :], ALU.subtract)
                dve.tensor_tensor(qrow[:, 4 * half:4 * half + 4, NOPE + 16:QD], rt[:, 2, :, :], rt[:, 3, :, :], ALU.add).then_inc(S("q_rope"), 1)

        def dve_softplus_in(dve, j):
            dve.wait_ge(S("dtr_rdy"), j + 1)
            dve.wait_ge(S("dt_rdy"), j)
            dve.tensor_tensor(dtw[:, 0, :], dtr[:, :], brow[:, BR_DTB:BR_DTB + H], ALU.add).then_inc(S("dt_raw"), 1)
            dve.wait_ge(S("dt_raw"), j + 1)
            dve.tensor_scalar(dtw[:, 4, :], dtw[:, 0, :], 0.0, None, ALU.max)
            dve.tensor_scalar(dtw[:, 5, :], dtw[:, 0, :], -1.0, None, ALU.mult).then_inc(S("dt_flip"), 1)
            dve.wait_ge(S("dt_flip"), j + 1)
            dve.tensor_tensor(dtw[:, 1, :], dtw[:, 0, :], dtw[:, 5, :], ALU.min).then_inc(S("dt_neg"), 1)

        def dve_softplus_out(dve, j):
            dve.wait_ge(S("dt_exp"), j + 1)
            dve.tensor_scalar(dtw[:, 3, :], dtw[:, 2, :], 1.0, None, ALU.add).then_inc(S("dt_one"), 1)
            dve.wait_ge(S("dt_one"), j + 1)
            dve.tensor_scalar(dtw[:, 7, :], dtw[:, 3, :], -1.0, None, ALU.add)
            dve.reciprocal(dtw[:, 8, :], dtw[:, 3, :]).then_inc(S("dt_s1"), 1)
            dve.wait_ge(S("dt_s1"), j + 1)
            dve.tensor_tensor(dtw[:, 9, :], dtw[:, 2, :], dtw[:, 7, :], ALU.subtract).then_inc(S("dt_s2"), 1)
            dve.wait_ge(S("dt_s2"), j + 1)
            dve.tensor_tensor(dtw[:, 10, :], dtw[:, 9, :], dtw[:, 8, :], ALU.mult).then_inc(S("dt_s3"), 1)
            dve.wait_ge(S("dt_s3"), j + 1)
            dve.wait_ge(S("dt_ln"), j + 1)
            dve.tensor_tensor(dtw[:, 11, :], dtw[:, 10, :], dtw[:, 6, :], ALU.add).then_inc(S("dt_s4"), 1)
            dve.wait_ge(S("dt_s4"), j + 1)
            dve.tensor_tensor(dt[:, :], dtw[:, 11, :], dtw[:, 4, :], ALU.add).then_inc(S("dt_rdy"), 1)
            dve.wait_ge(S("dt_rdy"), j + 1)
            dve.scalar_tensor_tensor(da[:, :], dt[:, :], -1.0, arow[:, :], ALU.mult, ALU.mult).then_inc(S("da_rdy"), 1)

        def dve_conv(dve, j, taps, out, done):
            for k in range(CK):
                if k:
                    dve.wait_ge(S("conv_step"), 3 * j + k)
                for c in range(CT):
                    w = cols[:, CO_CW + c * CK + k:CO_CW + c * CK + k + 1]
                    if k == 0:
                        last = dve.tensor_scalar(out(c), taps(c, k), w, cols[:, CO_CB + c:CO_CB + c + 1], ALU.mult, ALU.add)
                    else:
                        last = dve.scalar_tensor_tensor(out(c), taps(c, k), w, out(c), ALU.mult, ALU.add)
                last.then_inc(done if k == CK - 1 else S("conv_step"), 1)

        def dve_chunk_front(dve, j):
            dve.wait_ge(S("xraw_rdy"), 2 * j + 2)
            dve.wait_ge(S("xbcT_rdy"), j)
            dve_softplus_in(dve, j)
            dve_conv(dve, j, lambda c, k: xraw[:, c, k:k + P], lambda c: conv[:, c, :], S("conv_rdy"))
            dve.wait_ge(S("conv_rdy"), j + 1)
            dve.tensor_copy(xraw[:, :, 0:CK - 1], xraw[:, :, P:]).then_inc(S("hist_rdy"), 1)
            dve.wait_ge(S("st_mm"), j)
            dve_softplus_out(dve, j)

        def dve_chunk_mid(dve, j):
            dve.wait_ge(S("g_mm"), j + 1)
            dve.wait_ge(S("st_mm"), j)
            dve.tensor_copy(cd[:, 1:3, :], pb[:, 7, 0:2 * H].rearrange("p (a h) -> p a h", a=2)).then_inc(S("cs_rdy"), 1)
            dve.tensor_tensor(gm[:, :, :], pb[:, 7, P:3 * P].rearrange("p (g l) -> p g l", g=2), bc(tri, 1, [P, 2, P]), ALU.mult).then_inc(S("gm_rdy"), 1)
            dve.wait_ge(S("cs_rdy"), j + 1)
            dve.tensor_tensor(cd[:, 0, :], cd[:, 2, :], cd[:, 1, :], ALU.subtract).then_inc(S("cd_rdy"), 1)
            for half in range(2):
                dve.wait_ge(S("csb_mm"), 2 * j + 1 + half)
                for h in range(4 * half, 4 * half + 4):
                    last = dve.tensor_scalar(dd[:, h, :], pb[:, 2 + half, h % 4 * P:(h % 4 + 1) * P], cd[:, 1, h:h + 1], 0.0,
                                             ALU.subtract, ALU.min)
            last.then_inc(S("dd_rdy"), 1)
            dve.wait_ge(S("ew_rdy"), j + 1)
            dve.tensor_tensor(wend[:, :], ew[:, 0, :], dt[:, :], ALU.mult).then_inc(S("wend_rdy"), 1)
            dve.wait_ge(S("wend_rdy"), j + 1)
            dve.wait_ge(S("xr_rdy"), 2 * j + 1)
            dve.tensor_tensor(xw[:, :].rearrange("p (h d) -> p h d", h=H), xrow[:, :].rearrange("p (h d) -> p h d", h=H),
                              bc(wend[:, :], 2, [P, H, 64]), ALU.mult).then_inc(S("xw_rdy"), 1)
            dve.wait_ge(S("dexp_rdy"), j + 1)
            dve.wait_ge(S("gm_rdy"), j + 1)
            for h in range(H):
                last = dve.scalar_tensor_tensor(mT[:, h, :], mT[:, h, :], dt[:, h:h + 1], gm[:, h // 4, :], ALU.mult, ALU.mult)
            last.then_inc(S("mT_rdy"), 1)

        def dve_chunk_back(dve, j):
            hd = lambda ap: ap.rearrange("p (h d) -> p h d", h=H)
            dve.wait_ge(S("y_out"), j)
            dve.tensor_tensor(hd(yb[:, 0, :]), hd(xrow[:, :]), bc(brow[:, BR_DSK:BR_DSK + H], 2, [P, H, 64]), ALU.mult).then_inc(S("y_skip"), 1)
            dve.wait_ge(S("y_skip"), j + 1)
            dve.wait_ge(S("yd_mm"), j + 1)
            dve.tensor_tensor(yb[:, 1, :], pb[:, 7, :], yb[:, 0, :], ALU.add).then_inc(S("y_diag_used"), 1)
            dve.wait_ge(S("yo_mm"), j + 1)
            dve.tensor_tensor(hd(yb[:, 2, :]), hd(pb[:, 2, :]), bc(ew[:, 1, :], 2, [P, H, 64]), ALU.mult).then_inc(S("yo_used"), 1)
            dve.tensor_tensor(hd(st1[:, :]), hd(state[:, :]), bc(ew[:, 2, :], 2, [P, H, 64]), ALU.mult).then_inc(S("state_dec"), 1)
            dve.wait_ge(S("yo_used"), j + 1)
            dve.wait_ge(S("y_diag_used"), j + 1)
            dve.tensor_tensor(yb[:, 3, :], yb[:, 1, :], yb[:, 2, :], ALU.add).then_inc(S("y_sum"), 1)
            dve.wait_ge(S("st_mm"), j + 1)
            dve.wait_ge(S("state_dec"), j + 1)
            dve.tensor_tensor(state[:, :], pb[:, 3, :], st1[:, :], ALU.add).then_inc(S("state_rdy"), 1)
            dve.wait_ge(S("y_sum"), j + 1)
            dve.wait_ge(S("zs_rdy"), j + 1)
            dve.tensor_tensor(yb[:, 4, :], yb[:, 3, :], zs[:, :], ALU.mult).then_inc(S("y_rdy"), 1)

        def dve_decode(dve):
            j = TILES - 1
            hd = lambda ap: ap.rearrange("p (h d) -> p h d", h=H)
            dve.wait_ge(S("xraw_rdy"), 2 * TILES)
            dve.tensor_copy(lastraw[:, :, :], xraw[:, :, 0:CK - 1]).then_inc(S("last_raw"), 1)
            dve.wait_ge(S("cprev_in"), 16)
            dve.tensor_copy(cnew[:, :, 0:CK - 2, :], cprev[:, :, 1:CK - 1, :]).then_inc(S("cnew_rdy"), 1)
            dve.tensor_copy(cnew[:, :, CK - 2, :], xraw[:, :, CK - 1:CK - 1 + NB]).then_inc(S("cnew_rdy"), 1)
            dve_softplus_in(dve, j)
            dve.wait_ge(S("xbcT_rdy"), j)
            dve_conv(dve, j, lambda c, k: cprev[:, c, k, :] if k < CK - 1 else xraw[:, c, CK - 1:CK - 1 + NB],
                     lambda c: conv[:, c, 0:NB], S("conv_rdy"))
            dve.wait_ge(S("st_mm"), PT)
            dve_softplus_out(dve, j)
            dve.wait_ge(S("ew_rdy"), TILES)
            dve.tensor_tensor(decm[:, :, :], bc(ew[:, 0, :], 1, [P, NB, H]), bc(ident[:, 0:NB], 2, [P, NB, H]), ALU.mult).then_inc(S("decm_rdy"), 1)
            dve.wait_ge(S("xr_rdy"), 2 * j + 1)
            dve.tensor_tensor(hd(xdt[:, :]), hd(xrow[:, :]), bc(dt[:, :], 2, [P, H, 64]), ALU.mult).then_inc(S("xdt_rdy"), 1)
            dve.wait_ge(S("xbcT_rdy"), TILES)
            for g in range(2):
                last = dve.tensor_tensor(cm[:, g, :, :], bc(xbcT[:, 6 + g, 0:NB], 1, [P, NB, NB]),
                                         t_eye[:, :, :], ALU.mult)
            last.then_inc(S("cm_rdy"), 1)
            dve.wait_ge(S("xdt_rdy"), 1)
            dve.wait_ge(S("kv_mm"), 2 * TILES)
            for b in range(NB):
                dve.tensor_scalar(sx[:, b, :], xdt[:, :], ident[:, b:b + 1], None, ALU.mult).then_inc(S("sx_rdy"), 1)
            dve.wait_ge(S("sdec_mm"), 1)
            dve.tensor_copy(sdec[:, :], pb[:, 7, 0:NB * H]).then_inc(S("sdec_rdy"), 1)
            dve.wait_ge(S("sdec_rdy"), 1)
            dve.wait_ge(S("shist_in"), 16)
            for b in range(NB):
                dve.tensor_tensor(hd(st1[:, :]) if b % 2 else hd(xw[:, :]), hd(shist[:, b * 512:(b + 1) * 512]),
                                  bc(sdec[:, b * H:(b + 1) * H], 2, [P, H, 64]), ALU.mult).then_inc(S("sd_step"), 1)
                dve.wait_ge(S("sd_step"), b + 1)
                dve.wait_ge(S("bx_mm"), b + 1)
                dve.tensor_tensor(snew[:, b * 512:(b + 1) * 512], pb[:, 2 + b % 2, :], st1[:, :] if b % 2 else xw[:, :], ALU.add).then_inc(S("snew_rdy"), 1)
                if b < NB - 1:
                    dve.wait_ge(S("snew_rdy"), b + 1)
            dve.wait_ge(S("y_out"), j)
            dve.tensor_tensor(hd(yb[:, 0, :]), hd(xrow[:, :]), bc(brow[:, BR_DSK:BR_DSK + H], 2, [P, H, 64]), ALU.mult)
            dve.memset(yb[:, 1, :], 0.0).then_inc(S("y_skip"), 1)
            dve.wait_ge(S("y_skip"), j + 1)
            dve.wait_ge(S("ys_mm"), 1)
            dve.wait_ge(S("zs_rdy"), TILES)
            for g in range(2):
                last = dve.tensor_copy(yb[0:NB, 1, g * 256:(g + 1) * 256], pb[0:NB, 5 + g, 0:256])
            last.then_inc(S("y_diag_used"), 1)
            dve.wait_ge(S("y_diag_used"), j + 1)
            dve.tensor_tensor(yb[:, 3, :], yb[:, 0, :], yb[:, 1, :], ALU.add).then_inc(S("y_sum"), 1)
            dve.wait_ge(S("y_sum"), j + 1)
            dve.tensor_tensor(yb[:, 4, :], yb[:, 3, :], zs[:, :], ALU.mult).then_inc(S("y_rdy"), 1)

        @block.vector
        def _(dve):
            dve.memset(xraw[:, :, 0:CK - 1], 0.0).then_inc(S("hist_rdy"), 1)
            dve.memset(conv[:, :, :], 0.0).then_inc(S("conv_zero"), 1)
            dve.wait_ge(const_in, 3 * 16)
            dve_turned_x(dve, 0)
            dve.wait_ge(cs_in, 16)
            dve.wait_ge(S("a_exp"), 1)
            dve_latents(dve, 0)
            dve_turned_c(dve, 0)
            dve_rope_heads(dve, 0)
            dve.wait_ge(S("conv_zero"), 1)
            dve.wait_ge(S("ones_rdy"), 4)
            with dve.Fori(1, TILES) as i:
                dve_turned_x(dve, i)
                dve_chunk_front(dve, i - 1)
                dve_latents(dve, i)
                dve_chunk_mid(dve, i - 1)
                dve.wait_ge(S("k_st"), 16 * (i - 1))
                for half in range(2):
                    dve.wait_ge(S("k_tr"), 2 * i - 1 + half)
                    dve.tensor_copy(kT[:, 4 * half:4 * half + 4, :], T[half][0:QD, :].rearrange("p (h t) -> p h t", h=4)).then_inc(S("kT_rdy"), 1)
                dve_turned_c(dve, i)
                dve_rope_heads(dve, i)
                dve_chunk_back(dve, i - 1)
            dve_decode(dve)

        block.__exit__(None, None, None)
        p1.close()
        end_phase()


        p2 = ExitStack()
        att_rows = sb_in(p2, "att_rows", [P, TILES, H * VD])
        p23 = ExitStack()
        pages = [sb_in(p23, f"pages{n}", [P, PAGES, CACHE_W]) for n in range(2)]
        pt_sb = sb_in(p23, "pt_sb", [1, NB * PAGES], I32)
        ukt = sb_in(p23, "ukt", [NOPE, H, KL])
        p2a = ExitStack()
        qh = [sb_in(p2a, f"qh{n}", [QD, SEQ]) for n in range(2)]
        kh = [sb_in(p2a, f"kh{n}", [QD, SEQ]) for n in range(2)]
        vh = [sb_in(p2a, f"vh{n}", [P, PT, VD]) for n in range(2)]
        prob = [sb_in(p2a, f"prob{n}", [P, SEQ]) for n in range(2)]
        probT = [sb_in(p2a, f"probT{n}", [P, SEQ]) for n in range(2)]
        mx = sb_in(p2a, "mx", [P, 2])
        nmx = sb_in(p2a, "nmx", [P, 2])
        den = [sb_in(p2a, f"den{n}", [P, PT]) for n in range(2)]
        rden = [sb_in(p2a, f"rden{n}", [P, PT]) for n in range(2)]
        head_in = [S(f"head_in{n}") for n in range(2)]
        page_in = [[S(f"page_in{n}_{g}") for g in range(4)] for n in range(2)]

        STEPS = [(n, i) for n in range(2) for i in range(PT)]

        def sc(t):
            return pb[:, 2 * (t % 2):2 * (t % 2) + 2, :].rearrange("p a n -> p (a n)")

        def turned(dve, hp, t):
            w = min(512, (STEPS[t][1] + 1) * P)
            dve.wait_ge(S("p_tr"), G_BODY * hp + GROUPS[t] + 1)
            if t:
                dve.wait_ge(S("pv_step"), 16 * hp + t - 1)
            dve.tensor_copy(probT[t % 2][:, 0:w], pb[:, 4, 0:w]).then_inc(S("pT_rdy0"), 1)

        GROUPS = {t: sum(1 + (i >= 4) for _, i in STEPS[:t]) for t in range(16)}
        G_BODY = sum(1 + (i >= 4) for _, i in STEPS)
        LONG = [t for t, (_, i) in enumerate(STEPS) if i >= 4]

        def load_pages(sp, b, n, groups=range(4)):
            for g in groups:
                found = nc.values_load_multi_w_load_instructions(
                    pt_sb[0:1, bass.ds(b * PAGES + 8 * g, 8)], engines=(mybir.EngineType.SP,), min_val=0, max_val=cache.shape[0] - 1)[1]
                for m, page in enumerate(found):
                    sp.dma_start(pages[n][:, 8 * g + m, :],
                                 cache[bass.ds(page, 1), :, :].rearrange("a p w -> (a p) w")).then_inc(page_in[n][g], 16)

        block = nc.Block()
        block.__enter__()

        @block.sync
        def _(sp):
            sp.dma_start(pt_sb[:, :], page_table).then_inc(S("pt_in"), 16)
            sp.dma_start(ukt[:, :, :], t_in["w_ukt"]).then_inc(S("ukt_in"), 16)

            def load_head(hp, n):
                h = 2 * hp + n
                sp.dma_start(qh[n][:, :], qt_d[:, bass.ds(h, 1), 0:SEQ].rearrange("p a t -> p (a t)")).then_inc(head_in[n], 16)
                sp.dma_start(kh[n][:, :], kt_d[:, bass.ds(h, 1), 0:SEQ].rearrange("p a t -> p (a t)")).then_inc(head_in[n], 16)
                sp.dma_start(vh[n][:, :, :], v_d[0:SEQ, bass.ds(h * VD, VD)].rearrange("(t p) d -> p t d", p=P)).then_inc(head_in[n], 16)

            load_head(0, 0)
            load_head(0, 1)
            sp.wait_ge(S("pt_in"), 16)
            for hp in range(1, H // 2):
                for n in range(2):
                    sp.wait_ge(S("pv_step"), 16 * hp - 8 + 8 * n)
                    load_head(hp, n)
                    load_pages(sp, n, n, (hp - 1,))
            load_pages(sp, 0, 0, (3,))
            load_pages(sp, 1, 1, (3,))

        @block.tensor
        def _(pe):
            def scores(hp, t):
                n, i = STEPS[t]
                if i == 0:
                    pe.wait_ge(head_in[n], 48 * (hp + 1))
                if t >= 2:
                    pe.wait_ge(S("exp_rdy"), 16 * hp + t - 1)
                for a in range(0, (i + 1) * P, 512):
                    w = min(512, (i + 1) * P - a)
                    last = pe.matmul(pb[:, 2 * (t % 2) + a // 512, 0:w], qh[n][:, i * P:(i + 1) * P], kh[n][:, a:a + w], start=True, stop=True)
                last.then_inc(S("sc_mm"), 1)

            def turn(hp, t):
                n, i = STEPS[t]
                pe.wait_ge(S("exp_rdy"), 16 * hp + t + 1)
                for g in range(i // 4 + 1):
                    pe.wait_ge(S("pT_rdy0") if g == 0 else S("pT_rdy1"), 16 * hp + t if g == 0 else 8 * hp + LONG.index(t))
                    for m in range(4 * g, min(4 * g + 4, i + 1)):
                        last = pe.transpose(pb[:, 4 + g, m % 4 * P:(m % 4 + 1) * P], prob[t % 2][:, m * P:(m + 1) * P], ident)
                    last.then_inc(S("p_tr"), 1)

            def weigh(hp, t):
                n, i = STEPS[t]
                pe.wait_ge(S("pT_rdy0"), 16 * hp + t + 1)
                if i >= 4:
                    pe.wait_ge(S("pT_rdy1"), 8 * hp + LONG.index(t) + 1)
                if i == 0:
                    pe.wait_ge(S("att_rdy"), 2 * hp)
                for m in range(i + 1):
                    last = pe.matmul(pb[:, 6 + n, i * VD:(i + 1) * VD], probT[t % 2][:, m * P:(m + 1) * P], vh[n][:, m, :],
                                     start=m == 0, stop=m == i)
                last.then_inc(S("pv_step"), 1)

            with pe.Fori(0, H // 2) as hp:
                scores(hp, 0)
                for t in range(16):
                    if t < 15:
                        scores(hp, t + 1)
                    turn(hp, t)
                    if t:
                        weigh(hp, t - 1)
                weigh(hp, 15)

        @block.scalar
        def _(act):
            with act.Fori(0, H // 2) as hp:
                for t, (n, i) in enumerate(STEPS):
                    w = (i + 1) * P
                    act.wait_ge(S("nmx_rdy"), 16 * hp + t + 1)
                    if t >= 2:
                        act.wait_ge(S("p_tr"), G_BODY * hp + GROUPS[t - 1])
                    else:
                        act.wait_ge(S("p_tr"), G_BODY * hp)
                    act.activation(prob[t % 2][:, 0:w], sc(t)[:, 0:w], ACT.Exp, bias=nmx[:, t % 2:t % 2 + 1], scale=SCALE,
                                   accum_out=den[n][:, i:i + 1]).then_inc(S("exp_rdy"), 1)
                    if i >= 4:
                        act.wait_ge(S("p_tr"), G_BODY * hp + GROUPS[t] + 2)
                        act.wait_ge(S("pv_step"), 16 * hp + t - 1)
                        act.copy(probT[t % 2][:, 512:w], pb[:, 5, 0:w - 512]).then_inc(S("pT_rdy1"), 1)

        @block.vector
        def _(dve):
            def normalise(hp, n):
                dve.wait_ge(S("exp_rdy"), 16 * hp + 8 * n + 8)
                dve.reciprocal(rden[n][:, :], den[n][:, :]).then_inc(S("rden_rdy"), 1)
                dve.wait_ge(S("rden_rdy"), 2 * hp + n + 1)
                dve.wait_ge(S("pv_step"), 16 * hp + 8 * n + 8)
                dve.tensor_tensor(att_rows[:, 0:PT, bass.ds((2 * hp + n) * VD, VD)], pb[:, 6 + n, :].rearrange("p (t d) -> p t d", t=PT),
                                  bc(rden[n][:, :], 2, [P, PT, VD]), ALU.mult).then_inc(S("att_rdy"), 1)

            dve.memset(att_rows[:, PT, :], 0.0).then_inc(S("att_zero"), 1)
            with dve.Fori(0, H // 2) as hp:
                for t, (n, i) in enumerate(STEPS):
                    diag = sc(t)[:, i * P:(i + 1) * P]
                    dve.wait_ge(S("sc_mm"), 16 * hp + t + 1)
                    dve.tensor_tensor(diag, diag, cst[:, CS_CAUS:CS_CAUS + P], ALU.add).then_inc(S("masked"), 1)
                    dve.wait_ge(S("masked"), 16 * hp + t + 1)
                    dve.tensor_reduce(mx[:, t % 2:t % 2 + 1], sc(t)[:, 0:(i + 1) * P], AX.X, ALU.max).then_inc(S("mx_rdy"), 1)
                    dve.wait_ge(S("mx_rdy"), 16 * hp + t + 1)
                    if t:
                        dve.wait_ge(S("exp_rdy"), 16 * hp + t - 1)
                    dve.tensor_scalar(nmx[:, t % 2:t % 2 + 1], mx[:, t % 2:t % 2 + 1], -SCALE, None, ALU.mult).then_inc(S("nmx_rdy"), 1)
                    if t:
                        turned(dve, hp, t - 1)
                    if t == 10:
                        normalise(hp, 0)
                turned(dve, hp, 15)
                normalise(hp, 1)

        block.__exit__(None, None, None)
        p2a.close()
        end_phase("ukt_in", *[f"page_in{n}_{g}" for n in range(2) for g in range(4)])


        p3 = ExitStack()
        pages.append(sb_in(p3, "pages2", [P, PAGES, CACHE_W]))
        page_in.append([S(f"page_in2_{g}") for g in range(4)])
        qlat = sb_in(p3, "qlat", [P, 2, NB, H])
        qr4 = sb_in(p3, "qr4", [P, NB, 4, H])
        zq = [sb_in(p3, f"zq{n}", [P, 2, 56]) for n in range(2)]
        zr = [sb_in(p3, f"zr{n}", [P, 4 * H]) for n in range(2)]
        newT = sb_in(p3, "newT", [P, 3, P])
        krg = [sb_in(p3, f"krg{n}", [P, 8, 4, ROPE]) for n in range(2)]
        krT = sb_in(p3, "krT", [P, 4, 2, P])
        pgT = [sb_in(p3, f"pgT{n}", [P, 4, 2, 2, P]) for n in range(2)]
        snew_s = sb_in(p3, "snew_s", [H, P])
        smx = sb_in(p3, "smx", [P, 2])
        mrow = sb_in(p3, "mrow", [1, 16, H])
        colmx = sb_in(p3, "colmx", [H, 1])
        m8 = sb_in(p3, "m8", [1, H])
        nb = sb_in(p3, "nb", [P, 1])
        pexp = sb_in(p3, "pexp", [P, 3, P])
        rs = sb_in(p3, "rs", [P, 3])
        pT = [sb_in(p3, f"pT{n}", [P, 2 * P + H]) for n in range(2)]
        o_sb = sb_in(p3, "o_sb", [P, KL])
        srd = sb_in(p3, "srd", [P, H])
        olat = sb_in(p3, "olat", [P, 2, H, NB])
        NSTEP = 4

        block = nc.Block()
        block.__enter__()

        @block.sync
        def _(sp):
            for b in range(2, NB):
                if b >= 3:
                    sp.wait_ge(S("spv_mm"), b - 2)
                load_pages(sp, b, b % 3)

        @block.tensor
        def _(pe):
            pe.wait_ge(S("ukt_in"), 16)
            for c in range(2):
                for h in range(H):
                    last = pe.matmul(pb[:, 6, (c * H + h) * NB:(c * H + h + 1) * NB], ukt[:, h, c * P:(c + 1) * P], qT[0:NOPE, h, 0:NB],
                                     start=True, stop=True)
            last.then_inc(S("qlat_mm"), 1)
            for h in range(H):
                last = pe.transpose(pb[0:ROPE, 4 + h // 4, h % 4 * P:(h % 4 + 1) * P], qrow[:, h, NOPE:], ident)
            last.then_inc(S("qr_tr"), 1)
            pe.wait_ge(S("pad_rdy"), 1)
            for c in range(2):
                pe.transpose(pb[:, 7, c * P:(c + 1) * P], ckvn[:, c * P:(c + 1) * P], ident)
            pe.transpose(pb[0:ROPE, 7, 2 * P:3 * P], krn[:, :], ident).then_inc(S("new_tr"), 1)
            pe.wait_ge(S("qr_rdy"), 1)
            pe.wait_ge(S("newT_rdy"), 1)
            pe.wait_ge(S("o_zero"), 1)

            def turn_pages(b, n, m):
                pe.wait_ge(page_in[b % 3][m], 128 * (b // 3) + 128)
                for g in range(4):
                    if b or m:
                        pe.wait_ge(S("pgA") if g < 2 else S("pgV"), 9 * b + (2 * m - 1 + g % 2 if m else 0))
                    for c in range(2):
                        for half in range(2):
                            last = pe.transpose(pb[:, g, (2 * c + half) * P:(2 * c + half + 1) * P],
                                                pages[b % 3][:, 8 * m + 4 * half + g, c * P:(c + 1) * P], ident)
                    last.then_inc(S("pg_tr"), 1)

            def score_pages(b, n, m):
                pe.wait_ge(S("pgA"), 9 * b + 2 * m + 2)
                pe.wait_ge(S("pgV"), 9 * b + 2 * m + 2)
                for c in range(2):
                    for g in range(4):
                        last = pe.matmul(pb[32 * g:32 * g + 32, 4 + n, 0:2 * P], zq[n][:, c, 24 - 8 * m:56 - 8 * m],
                                         pgT[m % 2][:, g, c, :, :].rearrange("p a t -> p (a t)"),
                                         start=m == 0 and c == 0, stop=False, skip_group_check=True, tile_position=(0, 32 * g))
                last.then_inc(S("sp_mm"), 1)

            def turn_ropes(b, n):
                pe.wait_ge(S("krg_rdy"), 4 * b + 4)
                for q in range(2):
                    pe.wait_ge(S("pgA") if q == 0 else S("pgV"), 9 * b + 7)
                    for g in range(4):
                        last = pe.transpose(pb[:, 2 * q, g * P:(g + 1) * P], krg[n][:, 4 * q + g, :, :].rearrange("p m r -> p (m r)"), ident)
                    last.then_inc(S("kr_tr"), 1)

            def score_ropes(b, n):
                pe.wait_ge(S("pgA"), 9 * b + 9)
                pe.wait_ge(S("pgV"), 9 * b + 9)
                for g in range(4):
                    pe.matmul(pb[32 * g:32 * g + 32, 4 + n, 0:2 * P], zr[n][:, :], krT[:, g, :, :].rearrange("p a t -> p (a t)"),
                              start=False, stop=True, skip_group_check=True, tile_position=(0, 32 * g))
                at = pb[0:H, 4 + n, 2 * P:3 * P]
                for c in range(2):
                    pe.matmul(at, zq[n][:, c, 24:32], newT[:, c, :], start=c == 0, stop=False, skip_group_check=True)
                pe.matmul(at, zr[n][:, 0:H], newT[:, 2, :], start=False, stop=True, skip_group_check=True).then_inc(S("ss_mm"), 1)

            def scores(b, n):
                pe.wait_ge(S("zq_rdy"), 2 * b + 2)
                if b >= 2:
                    pe.wait_ge(S("sexp_rdy"), 2 * b - 2)
                for m in range(NSTEP):
                    turn_pages(b, n, m)
                    if m:
                        score_pages(b, n, m - 1)
                turn_ropes(b, n)
                score_pages(b, n, NSTEP - 1)
                score_ropes(b, n)

            def bounds(b):
                pe.wait_ge(S("smx_rdy"), b + 1)
                pe.transpose(pb[0:1, 6, 0:P], smx[:, 1:2], ident).then_inc(S("smx_tr"), 1)
                pe.wait_ge(S("mrow_rdy"), b + 1)
                pe.matmul(pb[:, 6, P:P + 1], mrow[:, :, :].rearrange("p a h -> p (a h)"), ones[0:1, 0:1], start=True, stop=True).then_inc(S("nb_mm"), 1)

            def weigh(b, n):
                pe.wait_ge(S("rs_rdy"), b + 1)
                pe.wait_ge(S("nb_rdy"), b + 1)
                pe.matmul(pb[:, 6, P + H:P + 2 * H], rs[:, 2:3].broadcast_to([P, P]), hsel, start=True, stop=True)
                for half in range(2):
                    pe.transpose(pb[:, 6, (2 + half) * P - 96:(3 + half) * P - 96], pexp[:, half, :], ident)
                pe.transpose(pb[:, 6, 4 * P - 96:4 * P - 96 + H], pexp[0:H, 2, :], ident[0:H, 0:H]).then_inc(S("pT_tr"), 1)
                pe.wait_ge(S("pT_rdy"), b + 1)
                if b:
                    pe.wait_ge(S("olat_rdy"), b)
                for x in range(PAGES + 1):
                    q = x % 4
                    if x < PAGES:
                        m, g8 = x // 8, x % 8
                        lhs = pT[n][:, (g8 // 4) * P + 32 * (g8 % 4) + 8 * m:(g8 // 4) * P + 32 * (g8 % 4) + 8 * m + 8]
                        last = pe.matmul(pb[32 * q:32 * q + H, 7, 0:KL], lhs, pages[b % 3][:, x, 0:KL], start=x < 4, stop=x >= PAGES - 4 and q > 0,
                                         skip_group_check=True, tile_position=(0, 32 * q))
                    else:
                        last = pe.matmul(pb[0:H, 7, 0:KL], pT[n][:, 2 * P:2 * P + H], ckvn[:, :], start=False, stop=True,
                                         skip_group_check=True, tile_position=(0, 0))
                last.then_inc(S("spv_mm"), 1)

            def latent(b):
                pe.wait_ge(S("o_rdy"), b + 1)
                for c in range(2):
                    last = pe.matmul(pb[:, 7, 2 * KL - 64 + c * H:2 * KL - 64 + (c + 1) * H], o_sb[:, c * P:(c + 1) * P], sel32, start=True, stop=True,
                                     skip_group_check=True)
                last.then_inc(S("olat_mm"), 1)

            scores(0, 0)
            for b in range(NB):
                bounds(b)
                if b + 1 < NB:
                    scores(b + 1, (b + 1) % 2)
                weigh(b, b % 2)
                latent(b)
            pe.wait_ge(S("olat_rdy"), NB)
            pe.wait_ge(S("sexp_rdy"), 2 * NB)
            for h in range(H):
                for c in range(2):
                    last = pe.matmul(pb[0:NB, 4, h * VD:(h + 1) * VD], olat[:, c, h, :], wkv[:, c, h * 2 * NOPE + NOPE:(h + 1) * 2 * NOPE],
                                     start=c == 0, stop=c == 1)
            last.then_inc(S("os_mm"), 1)

        @block.gpsimd
        def _(pool):
            for n in range(2):
                pool.memset(zq[n][:, :, :], 0.0).then_inc(S("zq_zero"), 1)
            pool.wait_ge(S("zq_zero"), 2)
            pool.wait_ge(S("qr_rdy"), 1)
            pool.wait_ge(S("qlat_rdy"), 1)
            for b in range(NB):
                n = b % 2
                if b >= 2:
                    pool.wait_ge(S("ss_mm"), b - 1)
                pool.tensor_copy(zq[n][:, :, 24:32], qlat[:, :, b, :]).then_inc(S("zq_rdy"), 1)
                pool.tensor_copy(zr[n][:, :], qr4[:, b, :, :].rearrange("p m h -> p (m h)")).then_inc(S("zq_rdy"), 1)
                for m in range(4):
                    pool.wait_ge(page_in[b % 3][m], 128 * (b // 3) + 128)
                    pool.tensor_copy(krg[n][:, :, m, :], pages[b % 3][:, 8 * m:8 * m + 8, KL:]).then_inc(S("krg_rdy"), 1)

        @block.scalar
        def _(act):
            def evacuate(b):
                for m in range(NSTEP):
                    if b or m >= 2:
                        act.wait_ge(S("sp_mm"), 4 * b + m - 1)
                    for g in (0, 1):
                        act.wait_ge(S("pg_tr"), 16 * b + 4 * m + g + 1)
                        act.copy(pgT[m % 2][:, g, :, :, :].rearrange("p c a t -> p (c a t)"), pb[:, g, :]).then_inc(S("pgA"), 1)
                act.wait_ge(S("kr_tr"), 2 * b + 1)
                if b:
                    act.wait_ge(S("ss_mm"), b)
                act.copy(krT[:, :, 0, :], pb[:, 0, :].rearrange("p (g t) -> p g t", g=4)).then_inc(S("pgA"), 1)

            def exps(b):
                act.wait_ge(S("nb_rdy"), b + 1)
                if b:
                    act.wait_ge(S("pT_tr"), b)
                act.activation(pexp[:, 0:2, :].rearrange("p a t -> p (a t)"), pb[:, 4 + b % 2, 0:2 * P], ACT.Exp, bias=nb[:, :], scale=SCALE,
                               accum_out=rs[:, 0:1]).then_inc(S("sexp_rdy"), 1)
                act.activation(pexp[0:H, 2, :], snew_s[:, :], ACT.Exp, bias=nb[0:H, :], scale=SCALE, accum_out=rs[0:H, 1:2]).then_inc(S("sexp_rdy"), 1)

            evacuate(0)
            for b in range(NB):
                exps(b)
                if b + 1 < NB:
                    evacuate(b + 1)

        @block.vector
        def _(dve):
            dve.memset(pb[:, 7, :], 0.0).then_inc(S("pad_rdy"), 1)
            dve.memset(qr4[:, :, :, :], 0.0).then_inc(S("qr_zero"), 1)
            dve.memset(rs[:, :], 0.0).then_inc(S("rs_zero"), 1)
            dve.wait_ge(S("qlat_mm"), 1)
            dve.tensor_copy(qlat[:, :, :, :], pb[:, 6, 0:2 * H * NB].rearrange("p (c h b) -> p c b h", c=2, h=H)).then_inc(S("qlat_rdy"), 1)
            dve.wait_ge(S("new_tr"), 1)
            dve.tensor_copy(newT[:, :, :], pb[:, 7, 0:3 * P].rearrange("p (c t) -> p c t", c=3)).then_inc(S("newT_rdy"), 1)
            dve.wait_ge(S("newT_rdy"), 1)
            dve.memset(pb[:, 7, :], 0.0).then_inc(S("o_zero"), 1)
            dve.wait_ge(S("qr_tr"), 1)
            dve.wait_ge(S("qr_zero"), 1)
            for m in range(4):
                for half in range(2):
                    last = dve.tensor_copy(qr4[32 * m:32 * m + 32, :, m, 4 * half:4 * half + 4],
                                           pb[0:ROPE, 4 + half, :].rearrange("p (h t) -> p t h", h=4)[:, 0:NB, :])
            last.then_inc(S("qr_rdy"), 1)

            def evacuate(b):
                for m in range(NSTEP):
                    if b or m >= 2:
                        dve.wait_ge(S("sp_mm"), 4 * b + m - 1)
                    for g in (2, 3):
                        dve.wait_ge(S("pg_tr"), 16 * b + 4 * m + g + 1)
                        dve.tensor_copy(pgT[m % 2][:, g, :, :, :].rearrange("p c a t -> p (c a t)"), pb[:, g, :]).then_inc(S("pgV"), 1)
                dve.wait_ge(S("kr_tr"), 2 * b + 2)
                if b:
                    dve.wait_ge(S("ss_mm"), b)
                dve.tensor_copy(krT[:, :, 1, :], pb[:, 2, :].rearrange("p (g t) -> p g t", g=4)).then_inc(S("pgV"), 1)

            def largest(b):
                dve.wait_ge(S("ss_mm"), b + 1)
                if b:
                    dve.wait_ge(S("smx_tr"), b)
                    dve.wait_ge(S("sexp_rdy"), 2 * b)
                dve.tensor_reduce(smx[:, 0:1], pb[:, 4 + b % 2, 0:2 * P], AX.X, ALU.max).then_inc(S("smx1"), 1)
                dve.tensor_tensor(snew_s[:, :], pb[0:H, 4 + b % 2, 2 * P:3 * P], cst[0:H, CS_NEG + 127 - b:CS_NEG + 255 - b], ALU.add).then_inc(S("snew1"), 1)
                dve.wait_ge(S("smx1"), b + 1)
                dve.tensor_copy(smx[:, 1:2], smx[:, 0:1]).then_inc(S("smx2"), 1)
                dve.wait_ge(S("snew1"), b + 1)
                dve.wait_ge(S("smx2"), b + 1)
                dve.tensor_reduce(colmx[:, :], snew_s[:, :], AX.X, ALU.max).then_inc(S("colmx_rdy"), 1)
                dve.wait_ge(S("colmx_rdy"), b + 1)
                dve.tensor_tensor(smx[0:H, 1:2], smx[0:H, 0:1], colmx[:, :], ALU.max).then_inc(S("smx_rdy"), 1)

            def row_bounds(b):
                dve.wait_ge(S("smx_tr"), b + 1)
                dve.tensor_reduce(m8[:, :], pb[0:1, 6, 0:P].rearrange("p (a h) -> p h a", h=H), AX.X, ALU.max).then_inc(S("m8_rdy"), 1)
                dve.wait_ge(S("m8_rdy"), b + 1)
                if b:
                    dve.wait_ge(S("nb_mm"), b)
                dve.tensor_scalar(mrow[:, :, :], bc(m8[:, :], 1, [1, 16, H]), -SCALE, None, ALU.mult).then_inc(S("mrow_rdy"), 1)
                dve.wait_ge(S("nb_mm"), b + 1)
                if b:
                    dve.wait_ge(S("sexp_rdy"), 2 * b)
                dve.tensor_copy(nb[:, :], pb[:, 6, P:P + 1]).then_inc(S("nb_rdy"), 1)

            def row_sums(b):
                dve.wait_ge(S("sexp_rdy"), 2 * b + 2)
                if b:
                    dve.wait_ge(S("pT_tr"), b)
                else:
                    dve.wait_ge(S("rs_zero"), 1)
                dve.tensor_tensor(rs[:, 2:3], rs[:, 0:1], rs[:, 1:2], ALU.add).then_inc(S("rs_rdy"), 1)

            def turned_probs(b):
                dve.wait_ge(S("pT_tr"), b + 1)
                if b >= 2:
                    dve.wait_ge(S("spv_mm"), b - 1)
                dve.tensor_copy(pT[b % 2][:, :], pb[:, 6, 2 * P - 96:4 * P - 96 + H]).then_inc(S("pT_rdy"), 1)
                if b:
                    dve.wait_ge(S("olat_rdy"), b)
                dve.reciprocal(srd[:, :], pb[:, 6, P + H:P + 2 * H]).then_inc(S("srd_rdy"), 1)

            def latent_out(b):
                dve.wait_ge(S("spv_mm"), b + 1)
                if b:
                    dve.wait_ge(S("olat_mm"), b)
                dve.tensor_copy(o_sb[:, :], pb[:, 7, 0:KL]).then_inc(S("o_rdy"), 1)
                dve.wait_ge(S("srd_rdy"), b + 1)
                dve.wait_ge(S("olat_mm"), b + 1)
                dve.tensor_tensor(olat[:, :, :, b], pb[:, 7, 2 * KL - 64:2 * KL - 64 + 2 * H].rearrange("p (c h) -> p c h", c=2),
                                  bc(srd[:, :], 1, [P, 2, H]), ALU.mult).then_inc(S("olat_rdy"), 1)

            evacuate(0)
            largest(0)
            for b in range(NB):
                row_bounds(b)
                if b + 1 < NB:
                    evacuate(b + 1)
                row_sums(b)
                turned_probs(b)
                if b + 1 < NB:
                    largest(b + 1)
                latent_out(b)
            dve.wait_ge(S("os_mm"), 1)
            dve.tensor_copy(att_rows[0:NB, PT, :], pb[0:NB, 4, :]).then_inc(S("att_dec"), 1)

        block.__exit__(None, None, None)
        p3.close()
        p23.close()
        end_phase()

        p4a = ExitStack()
        wout = sb_in(p4a, "wout", [P, KD, D])
        wr = sb_in(p4a, "wr", [P, KD, NG + NE])
        mixr = sb_in(p4a, "mixr", [P, D])
        mixT = sb_in(p4a, "mixT", [P, KD, P])
        xa = sb_in(p4a, "xa", [P, D])
        x2 = sb_in(p4a, "x2", [P, D])
        hn = sb_in(p4a, "hn", [P, D])
        hfT = sb_in(p4a, "hfT", [P, KD, P])
        asq = sb_in(p4a, "asq", [P, 512])
        st4 = sb_in(p4a, "st4", [P, 6])
        lg = sb_in(p4a, "lg", [P, TILES, NG + NE])
        gmax = sb_in(p4a, "gmax", [P, TILES])
        gexp = sb_in(p4a, "gexp", [P, TILES, NG])
        gsum = sb_in(p4a, "gsum", [P, TILES])
        gprob = sb_in(p4a, "gprob", [P, TILES])
        goh = sb_in(p4a, "goh", [P, TILES, NG])
        me = [sb_in(p4a, f"me{k}", [P, TILES, NE]) for k in range(2)]
        eq = sb_in(p4a, "eq", [P, TILES, NE])
        best = sb_in(p4a, "best", [P, TILES])
        emax = sb_in(p4a, "emax", [P, 2, TILES])
        ehot = [sb_in(p4a, f"ehot{k}", [P, TILES, NE]) for k in range(2)]
        eexp = sb_in(p4a, "eexp", [P, 2, TILES])
        ehs = sb_in(p4a, "ehs", [P, TILES, NE])
        esum = sb_in(p4a, "esum", [P, TILES + 1, NE])
        blk = sb_in(p4a, "blk", [P, NE, TILES])
        nblk = sb_in(p4a, "nblk", [P, NE])
        low = sb_in(p4a, "low", [P, NE, NE])
        first = sb_in(p4a, "first", [P, 3, NE])
        rank = sb_in(p4a, "rank", [P, TILES, NE])
        se = sb_in(p4a, "se", [P, SLOTS, NE])
        sef = sb_in(p4a, "sef", [P, 2, SLOTS])
        pr = [sb_in(p4a, f"pr{k}", [P, TILES, NE]) for k in range(2)]
        pos = sb_in(p4a, "pos", [P, 2, TILES])
        posc = sb_in(p4a, "posc", [P, 2, TILES])
        ge = sb_in(p4a, "ge", [P, 2 * TILES, SLOTS])
        pdiv = sb_in(p4a, "pdiv", [P, 2 * TILES])
        pmod = sb_in(p4a, "pmod", [P, 2 * TILES])
        tokv = sb_in(p4a, "tokv", [P, TILES])
        hotm = sb_in(p4a, "hotm", [P, 2 * TILES, P])
        hots = sb_in(p4a, "hots", [P, 2 * TILES, SLOTS])
        iota = lambda n: cst[:, CS_IOTA:CS_IOTA + n]

        block = nc.Block()
        block.__enter__()

        @block.sync
        def _(sp):
            sp.dma_start(mixr[:, 512:], ssm_d[0:P, :]).then_inc(S("ssm_in"), 16)
            sp.dma_start(xa[:, :], x_all[0:P, :]).then_inc(S("xa_in"), 16)
            wv = w_out.rearrange("(k p) n -> p k n", p=P)
            for half in range(2):
                sp.dma_start(wout[:, :, half * 512:(half + 1) * 512], wv[:, :, half * 512:(half + 1) * 512]).then_inc(S("wout_in"), 16)
            sp.dma_start(wr[:, :, :], w_rout.rearrange("(k p) n -> p k n", p=P)).then_inc(S("wr_in"), 16)

            def stores(i):
                sp.wait_ge(S("x2_rdy"), 2 * i + 2)
                sp.dma_start(x2_d[bass.ds(i * P, P), :], x2[:, :]).then_inc(S("x2_st"), 16)
                if not isinstance(i, int):
                    sp.dma_start(xa[:, :], x_all[bass.ds(i * P + P, P), :]).then_inc(S("xa_in"), 16)
                sp.wait_ge(S("hn_rdy"), i + 1)
                sp.dma_start(hn_d[bass.ds(i * P, P), :], hn[:, :]).then_inc(S("hn_st"), 16)

            with sp.Fori(0, TILES - 1) as i:
                sp.wait_ge(S("mix_tr"), 2 * i + 2)
                sp.dma_start(mixr[:, 512:], ssm_d[bass.ds(i * P + P, P), :]).then_inc(S("ssm_in"), 16)
                stores(i)
            stores(TILES - 1)
            sp.wait_ge(S("x2_st"), 16 * TILES)
            sp.wait_ge(S("hn_st"), 16 * TILES)

        @block.tensor
        def _(pe):
            def turn_mix(i):
                pe.wait_ge(S("mix_a"), i + 1)
                pe.wait_ge(S("ssm_in"), 16 * i + 16)
                if later(i):
                    pe.wait_ge(S("mixT_rdy"), 2 * i)
                for half in range(2):
                    for k in range(4):
                        last = pe.transpose(pb[:, half, k * P:(k + 1) * P], mixr[:, (4 * half + k) * P:(4 * half + k + 1) * P], ident)
                    last.then_inc(S("mix_tr"), 1)

            def project(i):
                pe.wait_ge(S("mixT_rdy"), 2 * i + 2)
                if later(i):
                    pe.wait_ge(S("x2_rdy"), 2 * i)
                else:
                    pe.wait_ge(S("wout_in"), 32)
                for half in range(2):
                    for k in range(KD):
                        last = pe.matmul(pb[:, 2 + half, :], mixT[:, k, :], wout[:, k, half * 512:(half + 1) * 512], start=k == 0, stop=k == KD - 1)
                    last.then_inc(S("out_mm"), 1)

            def route(i):
                pe.wait_ge(S("hn_rdy"), i + 1)
                if later(i):
                    pe.wait_ge(S("hfT_rdy"), 2 * i)
                for half in range(2):
                    for k in range(4):
                        last = pe.transpose(pb[:, 4 + half, k * P:(k + 1) * P], hn[:, (4 * half + k) * P:(4 * half + k + 1) * P], ident)
                    last.then_inc(S("h_tr"), 1)
                pe.wait_ge(S("hfT_rdy"), 2 * i + 2)
                if later(i):
                    pe.wait_ge(S("lg_rdy"), i)
                else:
                    pe.wait_ge(S("wr_in"), 16)
                for k in range(KD):
                    last = pe.matmul(pb[:, 6, 0:NG + NE], hfT[:, k, :], wr[:, k, :], start=k == 0, stop=k == KD - 1)
                last.then_inc(S("r_mm"), 1)

            turn_mix(0)
            project(0)
            turn_mix(1)
            with pe.Fori(1, TILES - 1) as i:
                project(i)
                turn_mix(i + 1)
                route(i - 1)
            project(TILES - 1)
            route(TILES - 2)
            route(TILES - 1)
            pe.wait_ge(S("esum_step"), TILES + 1)
            pe.matmul(pb[:, 6, 0:TILES * NE], tri, ehs[:, :, :].rearrange("p t e -> p (t e)"), start=True, stop=False)
            pe.matmul(pb[:, 6, 0:TILES * NE], ones[:, :], esum[:, 0:TILES, :].rearrange("p t e -> p (t e)"), start=False, stop=True)
            pe.matmul(pb[:, 6, 256:256 + NE], ones[:, :], esum[:, TILES, :], start=True, stop=True).then_inc(S("rank_mm"), 1)
            pe.wait_ge(S("hots_rdy"), 2)
            for c in range(2 * TILES):
                last = pe.matmul(pb[:, 7, 0:SLOTS], hotm[:, c, :], hots[:, c, :], start=c == 0, stop=c == 2 * TILES - 1)
            last.then_inc(S("tok_mm"), 1)

        @block.gpsimd
        def _(pool):
            def inverse_root(i, at, name, used):
                pool.wait_ge(S(name + "_sq"), i + 1)
                if later(i):
                    pool.wait_ge(S(used), i)
                pool.tensor_tensor(st4[:, at + 1:at + 2], st4[:, at:at + 1], meps[:, 0:1], ALU.add).then_inc(S(name + "_var"), 1)
                pool.wait_ge(S(name + "_var"), i + 1)
                pool.tensor_tensor(st4[:, at + 2:at + 3], st4[:, at + 1:at + 2], mhalf[:, 0:1], ALU.pow).then_inc(S(name + "_rs"), 1)

            inverse_root(0, 0, "a", "mix_a")
            with pool.Fori(0, TILES - 1) as i:
                inverse_root(i + 1, 0, "a", "mix_a")
                inverse_root(i, 3, "h", "hn_rdy")
            inverse_root(TILES - 1, 3, "h", "hn_rdy")

        @block.scalar
        def _(act):
            def mixer_rows(i):
                if later(i):
                    act.wait_ge(S("a_rs"), i)
                    act.wait_ge(S("mix_a"), i)
                act.activation(asq[:, :], att_rows[:, bass.ds(i, 1), :].rearrange("p a n -> p (a n)"), ACT.Square, scale=INNER ** -0.5,
                               accum_out=st4[:, 0:1]).then_inc(S("a_sq"), 1)
                act.wait_ge(S("a_rs"), i + 1)
                if later(i):
                    act.wait_ge(S("mix_tr"), 2 * i)
                    act.wait_ge(S("act_mark"), i)
                act.activation(amark[:, :], meps[:, 0:1], ACT.Copy).then_inc(S("act_mark"), 1)
                act.activation(mixr[:, 0:512], att_rows[:, bass.ds(i, 1), :].rearrange("p a n -> p (a n)"), ACT.Copy, scale=st4[:, 2:3]).then_inc(S("mix_a"), 1)

            def norm_rows(i):
                act.wait_ge(S("x2_rdy"), 2 * i + 2)
                if later(i):
                    act.wait_ge(S("h_rs"), i)
                    act.wait_ge(S("h_tr"), 2 * i)
                    act.wait_ge(S("hn_st"), 16 * i)
                act.activation(hn[:, :], x2[:, :], ACT.Square, scale=D ** -0.5, accum_out=st4[:, 3:4]).then_inc(S("h_sq"), 1)
                act.wait_ge(S("h_rs"), i + 1)
                act.activation(hn[:, :], x2[:, :], ACT.Copy, scale=st4[:, 5:6]).then_inc(S("hn_rdy"), 1)

            mixer_rows(0)
            with act.Fori(0, TILES - 1) as i:
                mixer_rows(i + 1)
                norm_rows(i)
            norm_rows(TILES - 1)
            act.wait_ge(S("gd_rdy"), 1)
            act.activation(gexp[:, :, :], gexp[:, :, :], ACT.Exp).then_inc(S("gexp_rdy"), 1)
            act.wait_ge(S("ed_rdy"), 1)
            act.activation(eexp[:, 1, :], eexp[:, 0, :], ACT.Exp).then_inc(S("eexp_rdy"), 1)

        @block.vector
        def _(dve):
            def turned_mix(i):
                for half in range(2):
                    dve.wait_ge(S("mix_tr"), 2 * i + 1 + half)
                    if half == 0 and later(i):
                        dve.wait_ge(S("out_mm"), 2 * i)
                    dve.tensor_tensor(mixT[:, 4 * half:4 * half + 4, :], pb[:, half, :].rearrange("p (k t) -> p k t", k=4),
                                      bc(cols[:, CO_GOUT + 4 * half:CO_GOUT + 4 * half + 4], 2, [P, 4, P]), ALU.mult).then_inc(S("mixT_rdy"), 1)

            def residual(i):
                dve.wait_ge(S("xa_in"), 16 * i + 16)
                if later(i):
                    dve.wait_ge(S("x2_st"), 16 * i)
                    dve.wait_ge(S("hn_rdy"), i)
                for half in range(2):
                    a = slice(half * 512, (half + 1) * 512)
                    dve.wait_ge(S("out_mm"), 2 * i + 1 + half)
                    dve.tensor_tensor(x2[:, a], pb[:, 2 + half, :], xa[:, a], ALU.add).then_inc(S("x2_rdy"), 1)

            def turned_h(i):
                for half in range(2):
                    dve.wait_ge(S("h_tr"), 2 * i + 1 + half)
                    if half == 0 and later(i):
                        dve.wait_ge(S("r_mm"), i)
                    dve.tensor_tensor(hfT[:, 4 * half:4 * half + 4, :], pb[:, 4 + half, :].rearrange("p (k t) -> p k t", k=4),
                                      bc(cols[:, CO_GFFN + 4 * half:CO_GFFN + 4 * half + 4], 2, [P, 4, P]), ALU.mult).then_inc(S("hfT_rdy"), 1)

            def logits(i):
                dve.wait_ge(S("r_mm"), i + 1)
                dve.tensor_tensor(lg[:, bass.ds(i, 1), :].rearrange("p a n -> p (a n)"), pb[:, 6, 0:NG + NE], brow[:, BR_RB:BR_RB + NG + NE],
                                  ALU.add).then_inc(S("lg_rdy"), 1)

            turned_mix(0)
            residual(0)
            turned_mix(1)
            with dve.Fori(1, TILES - 1) as i:
                residual(i)
                turned_mix(i + 1)
                turned_h(i - 1)
                logits(i - 1)
            residual(TILES - 1)
            for i in (TILES - 2, TILES - 1):
                turned_h(i)
                logits(i)

            rev = lambda n: bc(cst[:, CS_REV:CS_REV + n], 1, [P, TILES, n])
            dve.wait_ge(S("lg_rdy"), TILES)
            dve.tensor_reduce(gmax[:, :], lg[:, :, 0:NG], AX.X, ALU.max).then_inc(S("gmax_rdy"), 1)
            dve.wait_ge(S("gmax_rdy"), 1)
            dve.tensor_tensor(gexp[:, :, :], lg[:, :, 0:NG], bc(gmax[:, :], 2, [P, TILES, NG]), ALU.subtract).then_inc(S("gd_rdy"), 1)
            dve.tensor_tensor(goh[:, :, :], lg[:, :, 0:NG], bc(gmax[:, :], 2, [P, TILES, NG]), ALU.is_equal).then_inc(S("geq_rdy"), 1)
            dve.wait_ge(S("geq_rdy"), 1)
            dve.tensor_tensor(goh[:, :, :], goh[:, :, :], rev(NG), ALU.mult).then_inc(S("grev_rdy"), 1)
            dve.wait_ge(S("grev_rdy"), 1)
            dve.tensor_reduce(best[:, :], goh[:, :, :], AX.X, ALU.max).then_inc(S("gbest_rdy"), 1)
            dve.wait_ge(S("gbest_rdy"), 1)
            dve.tensor_tensor(goh[:, :, :], goh[:, :, :], bc(best[:, :], 2, [P, TILES, NG]), ALU.is_equal).then_inc(S("goh_rdy"), 1)
            dve.wait_ge(S("goh_rdy"), 1)
            dve.tensor_scalar(goh[:, :, :], goh[:, :, :], -1.0, -NEG, ALU.add, ALU.mult).then_inc(S("gpen_rdy"), 1)
            dve.wait_ge(S("gpen_rdy"), 1)
            for t in range(TILES):
                last = dve.tensor_tensor(me[0][:, t, :].rearrange("p (g e) -> p g e", g=NG), lg[:, t, NG:].rearrange("p (g e) -> p g e", g=NG),
                                         bc(goh[:, t, :], 2, [P, NG, EPG]), ALU.add)
            last.then_inc(S("me_rdy"), 1)
            for k in range(2):
                dve.wait_ge(S("me_rdy"), k + 1)
                if k:
                    dve.wait_ge(S("ehot_rdy"), k)
                dve.tensor_reduce(emax[:, k, :], me[k][:, :, :], AX.X, ALU.max).then_inc(S("emax_rdy"), 1)
                dve.wait_ge(S("emax_rdy"), k + 1)
                dve.tensor_tensor(eq[:, :, :], me[k][:, :, :], bc(emax[:, k, :], 2, [P, TILES, NE]), ALU.is_equal).then_inc(S("eeq_rdy"), 1)
                dve.wait_ge(S("eeq_rdy"), k + 1)
                dve.tensor_tensor(eq[:, :, :], eq[:, :, :], rev(NE), ALU.mult).then_inc(S("erev_rdy"), 1)
                dve.wait_ge(S("erev_rdy"), k + 1)
                dve.tensor_reduce(best[:, :], eq[:, :, :], AX.X, ALU.max).then_inc(S("ebest_rdy"), 1)
                dve.wait_ge(S("ebest_rdy"), k + 1)
                dve.tensor_tensor(ehot[k][:, :, :], eq[:, :, :], bc(best[:, :], 2, [P, TILES, NE]), ALU.is_equal).then_inc(S("ehot_rdy"), 1)
                if k == 0:
                    dve.wait_ge(S("ehot_rdy"), 1)
                    dve.scalar_tensor_tensor(me[1][:, :, :], ehot[0][:, :, :], NEG, me[0][:, :, :], ALU.mult, ALU.add).then_inc(S("me_rdy"), 1)
            dve.tensor_tensor(eexp[:, 0, :], emax[:, 1, :], emax[:, 0, :], ALU.subtract).then_inc(S("ed_rdy"), 1)
            dve.wait_ge(S("ehot_rdy"), 2)
            dve.tensor_tensor(ehs[:, :, :], ehot[0][:, :, :], ehot[1][:, :, :], ALU.add).then_inc(S("ehs_rdy"), 1)
            dve.memset(esum[:, 0, :], 0.0).then_inc(S("esum_step"), 1)
            dve.wait_ge(S("ehs_rdy"), 1)
            dve.tensor_scalar(ehs[:, PT, :], ehs[:, PT, :], cst[:, CS_VALID:CS_VALID + 1], None, ALU.mult).then_inc(S("ehs_rdy"), 1)
            dve.wait_ge(S("ehs_rdy"), 2)
            for t in range(TILES):
                dve.wait_ge(S("esum_step"), t + 1)
                dve.tensor_tensor(esum[:, t + 1, :], esum[:, t, :], ehs[:, t, :], ALU.add).then_inc(S("esum_step"), 1)
            dve.wait_ge(S("gexp_rdy"), 1)
            dve.tensor_reduce(gsum[:, :], gexp[:, :, :], AX.X, ALU.add).then_inc(S("gsum_rdy"), 1)
            dve.wait_ge(S("eexp_rdy"), 1)
            dve.tensor_scalar(best[:, :], eexp[:, 1, :], 1.0, None, ALU.add).then_inc(S("esum1_rdy"), 1)
            dve.wait_ge(S("gsum_rdy"), 1)
            dve.wait_ge(S("esum1_rdy"), 1)
            dve.tensor_tensor(gprob[:, :], gsum[:, :], best[:, :], ALU.mult).then_inc(S("gprob_rdy"), 1)
            dve.wait_ge(S("gprob_rdy"), 1)
            dve.reciprocal(gates[:, 0, :], gprob[:, :]).then_inc(S("gates_rdy"), 1)
            dve.wait_ge(S("gates_rdy"), 1)
            dve.tensor_tensor(gates[:, 1, :], gates[:, 0, :], eexp[:, 1, :], ALU.mult).then_inc(S("gates_rdy"), 1)
            dve.wait_ge(S("rank_mm"), 1)
            dve.tensor_copy(rank[:, :, :], pb[:, 6, 0:TILES * NE].rearrange("p (t e) -> p t e", t=TILES)).then_inc(S("rank_rdy"), 1)
            dve.tensor_scalar(nblk[:, :], pb[:, 6, 256:256 + NE], 1.0 / P, None, ALU.mult).then_inc(S("nfrac_rdy"), 1)
            dve.wait_ge(S("nfrac_rdy"), 1)
            dve.tensor_tensor(blk[:, :, :], bc(nblk[:, :], 2, [P, NE, TILES]), bc(iota(TILES), 1, [P, NE, TILES]), ALU.is_gt).then_inc(S("blk_rdy"), 1)
            dve.wait_ge(S("blk_rdy"), 1)
            dve.tensor_reduce(nblk[:, :], blk[:, :, :], AX.X, ALU.add).then_inc(S("nblk_rdy"), 1)
            dve.wait_ge(S("nblk_rdy"), 1)
            dve.tensor_tensor(low[:, :, :], cst[:, CS_LOW:CS_LOW + NE * NE].rearrange("p (a b) -> p a b", a=NE), bc(nblk[:, :], 1, [P, NE, NE]),
                              ALU.mult).then_inc(S("low_rdy"), 1)
            dve.wait_ge(S("low_rdy"), 1)
            dve.tensor_reduce(first[:, 0, :], low[:, :, :], AX.X, ALU.add).then_inc(S("first_rdy"), 1)
            dve.wait_ge(S("first_rdy"), 1)
            dve.tensor_tensor(first[:, 1, :], first[:, 0, :], nblk[:, :], ALU.add).then_inc(S("after_rdy"), 1)
            dve.tensor_scalar(first[:, 2, :], first[:, 0, :], float(P), -1.0, ALU.mult, ALU.add).then_inc(S("base_rdy"), 1)
            dve.wait_ge(S("after_rdy"), 1)
            dve.tensor_tensor(se[:, :, :], bc(first[:, 1, :], 1, [P, SLOTS, NE]), bc(iota(SLOTS), 2, [P, SLOTS, NE]), ALU.is_le).then_inc(S("se_rdy"), 1)
            dve.wait_ge(S("se_rdy"), 1)
            dve.tensor_reduce(sef[:, 0, :], se[:, :, :], AX.X, ALU.add).then_inc(S("sef_rdy"), 1)
            dve.wait_ge(S("sef_rdy"), 1)
            dve.tensor_scalar(sef[:, 1, :], sef[:, 0, :], float(NE - 1), None, ALU.min).then_inc(S("sef_rdy"), 1)
            dve.wait_ge(S("sef_rdy"), 2)
            dve.tensor_copy(slot_e[:, :], sef[:, 1, :]).then_inc(S("slot_rdy"), 1)
            dve.wait_ge(S("rank_rdy"), 1)
            dve.wait_ge(S("base_rdy"), 1)
            dve.tensor_tensor(rank[:, :, :], rank[:, :, :], bc(first[:, 2, :], 1, [P, TILES, NE]), ALU.add).then_inc(S("rank_rdy"), 1)
            dve.wait_ge(S("rank_rdy"), 2)
            for k in range(2):
                dve.tensor_tensor(pr[k][:, :, :], rank[:, :, :], ehot[k][:, :, :], ALU.mult).then_inc(S("pr_rdy"), 1)
                dve.wait_ge(S("pr_rdy"), k + 1)
                dve.tensor_reduce(pos[:, k, :], pr[k][:, :, :], AX.X, ALU.add).then_inc(S("pos_rdy"), 1)
            dve.wait_ge(S("pos_rdy"), 2)
            dve.tensor_scalar(posc[:, :, :], pos[:, :, :], 0.0, None, ALU.max).then_inc(S("posc_rdy"), 1)
            dve.wait_ge(S("posc_rdy"), 1)
            dve.tensor_copy(posg[:, :, :], posc[:, :, :]).then_inc(S("posg_rdy"), 1)
            posf = posc[:, :, :].rearrange("p k t -> p (k t)")
            dve.tensor_scalar(pmod[:, :], posf, 1.0 / P, None, ALU.mult).then_inc(S("pfrac_rdy"), 1)
            dve.wait_ge(S("pfrac_rdy"), 1)
            dve.tensor_tensor(ge[:, :, 0:SLOTS - 1], bc(pmod[:, :], 2, [P, 2 * TILES, SLOTS - 1]),
                              bc(cst[:, CS_IOTA + 1:CS_IOTA + SLOTS], 1, [P, 2 * TILES, SLOTS - 1]), ALU.is_ge).then_inc(S("ge_rdy"), 1)
            dve.wait_ge(S("ge_rdy"), 1)
            dve.tensor_reduce(pdiv[:, :], ge[:, :, 0:SLOTS - 1], AX.X, ALU.add).then_inc(S("pdiv_rdy"), 1)
            dve.wait_ge(S("pdiv_rdy"), 1)
            dve.scalar_tensor_tensor(pmod[:, :], pdiv[:, :], -float(P), posf, ALU.mult, ALU.add).then_inc(S("pmod_rdy"), 1)
            dve.tensor_tensor(ge[:, :, :], bc(pdiv[:, :], 2, [P, 2 * TILES, SLOTS]), bc(iota(SLOTS), 1, [P, 2 * TILES, SLOTS]),
                              ALU.is_equal).then_inc(S("gs_rdy"), 1)
            dve.tensor_copy(tokv[:, 0:PT], cst[:, CS_TOK:CS_TOK + PT])
            dve.tensor_tensor(tokv[:, PT:], cst[:, CS_TOK + PT:CS_TOK + TILES], cst[:, CS_VALID:CS_VALID + 1], ALU.mult).then_inc(S("tokv_rdy"), 1)
            dve.wait_ge(S("gs_rdy"), 1)
            dve.wait_ge(S("tokv_rdy"), 1)
            for k in range(2):
                last = dve.tensor_tensor(hots[:, k * TILES:(k + 1) * TILES, :], ge[:, k * TILES:(k + 1) * TILES, :],
                                         bc(tokv[:, :], 2, [P, TILES, SLOTS]), ALU.mult)
            last.then_inc(S("hots_rdy"), 1)
            dve.wait_ge(S("pmod_rdy"), 1)
            dve.tensor_tensor(hotm[:, :, :], bc(pmod[:, :], 2, [P, 2 * TILES, P]), bc(iota(P), 1, [P, 2 * TILES, P]), ALU.is_equal).then_inc(S("hots_rdy"), 1)
            dve.wait_ge(S("tok_mm"), 1)
            dve.tensor_copy(tokx[:, :], pb[:, 7, 0:SLOTS]).then_inc(S("tokx_rdy"), 1)

        block.__exit__(None, None, None)
        p4a.close()
        p2.close()
        mixer.close()
        end_phase()

        p5 = ExitStack()
        F32R = mybir.dt.float32r
        SHAPES = {"gate": [P, KD, FF], "up": [P, KD, FF], "down": [P, KF, D]}
        raw, high, low_ = [{w: sb_in(p5, f"{part}_{w}", shape, dt) for w, shape in SHAPES.items()}
                           for part, dt in (("raw", F32), ("high", F32R), ("low", F32R))]
        tix = sb_in(p5, "tix", [P, 1], U32)
        hx = sb_in(p5, "hx", [P, D])
        hxT = sb_in(p5, "hxT", [P, KD, P])
        hxH, hxL = [sb_in(p5, n, [P, KD, P], F32R) for n in ("hxH", "hxL")]
        sg = sb_in(p5, "sg", [P, FF])
        ax = sb_in(p5, "ax", [P, FF])
        axT = sb_in(p5, "axT", [P, KF, P])
        axH, axL = [sb_in(p5, n, [P, KF, P], F32R) for n in ("axH", "axL")]
        yo = sb_in(p5, "yo", [P, D])
        w_dram = {"gate": t_in["w_gate"], "up": t_in["w_up"], "down": t_in["w_down"]}
        rows_of = {"gate": D, "up": D, "down": FF}
        w_pg, w_pp, p_rows = [t_in[n] for n in ("w_pg", "w_pp", "p_t")]

        def part(ap, c):
            n = ap.shape[1] // 2
            return ap[:, c * n:(c + 1) * n, :].rearrange("p k n -> p (k n)")

        block = nc.Block()
        block.__enter__()

        @block.sync
        def _(sp):
            def store(slot):
                sp.wait_ge(S("yo_rdy"), 2 * slot + 2)
                sp.dma_start(y_d[bass.ds(slot * P, P), :], yo[:, :]).then_inc(S("yo_st"), 16)

            def load(slot, w, e):
                sp.dma_start(raw[w][:, :, :], w_dram[w][bass.ds(e * rows_of[w], rows_of[w]), :].rearrange("(k p) n -> p k n", p=P)).then_inc(S(w + "_in"), 16)

            def after_last(slot, w):
                if w == "down" and not isinstance(slot, int):
                    store(slot - 2)
                sp.wait_ge(S(w + "_low"), 2 * slot)

            def load_expert(slot):
                before, e = nc.values_load_multi_w_load_instructions(
                    slot_e[0:1, bass.ds(slot - 1, 2)], engines=(mybir.EngineType.SP,), min_val=0, max_val=NE - 1)[1]
                with sp.If(e != before):
                    for w in SHAPES:
                        after_last(slot, w)
                        load(slot, w, e)
                with sp.Else():
                    for w in SHAPES:
                        after_last(slot, w)
                        sp.sem_inc(S(w + "_in"), 16)

            first_e = nc.values_load_multi_w_load_instructions(
                slot_e[0:1, 0:1], engines=(mybir.EngineType.SP,), min_val=0, max_val=NE - 1)[1][0]
            for w in SHAPES:
                load(0, w, first_e)
            load_expert(1)
            with sp.Fori(2, SLOTS) as slot:
                load_expert(slot)
            store(SLOTS - 2)
            store(SLOTS - 1)
            sp.wait_ge(S("yo_st"), 16 * SLOTS)

        @block.gpsimd
        def _(pool):
            def gather(slot):
                pool.wait_ge(S("tix_rdy"), slot + 1)
                if later(slot):
                    pool.wait_ge(S("hx_tr"), 2 * slot)
                    pool.wait_ge(S("mark_rdy"), slot)
                    pool.tensor_tensor(mark[:, :], meps[:, 0:1], meps[:, 0:1], ALU.add).then_inc(S("mark_rdy"), 1)
                pool.indirect_dma_start(out=hx[:, :], out_offset=None, in_=hn_d[:, :],
                                        in_offset=bass.IndirectOffsetOnAxis(ap=tix[:, 0:1], axis=0)).then_inc(S("hx_in"), 16)

            pool.memset(mark[:, :], 0.0).then_inc(S("mark_rdy"), 1)
            gather(0)
            with pool.Fori(1, SLOTS) as slot:
                gather(slot)

        @block.tensor
        def _(pe):
            def turn_rows(slot):
                pe.wait_ge(S("hx_in"), 16 * slot + 16)
                if later(slot):
                    pe.wait_ge(S("hxT_rdy"), 2 * slot)
                for half in range(2):
                    for k in range(4):
                        last = pe.transpose(pb[:, half, k * P:(k + 1) * P], hx[:, (4 * half + k) * P:(4 * half + k + 1) * P], ident)
                    last.then_inc(S("hx_tr"), 1)

            def split_product(out, xh, xl, w, a, b):
                kt = xh.shape[1]
                for k in range(kt):
                    pe.matmul(out, xh[:, k, :], high[w][:, k, a:b], start=k == 0, stop=False)
                    pe.matmul(out, xh[:, k, :], low_[w][:, k, a:b], start=False, stop=False)
                    last = pe.matmul(out, xl[:, k, :], high[w][:, k, a:b], start=False, stop=k == kt - 1)
                return last

            def gate_up(slot):
                pe.wait_ge(S("hxL_rdy"), slot + 1)
                if later(slot):
                    pe.wait_ge(S("ax_rdy"), slot)
                for bank, w in ((2, "gate"), (3, "up")):
                    pe.wait_ge(S(w + "_low"), 2 * slot + 2)
                    split_product(pb[:, bank, :], hxH, hxL, w, 0, FF).then_inc(S(w + "_mm"), 1)

            def turn_product(slot):
                pe.wait_ge(S("ax_rdy"), slot + 1)
                if later(slot):
                    pe.wait_ge(S("axT_rdy"), slot)
                for k in range(KF):
                    last = pe.transpose(pb[:, 4, k * P:(k + 1) * P], ax[:, k * P:(k + 1) * P], ident)
                last.then_inc(S("ax_tr"), 1)

            def down(slot):
                pe.wait_ge(S("axL_rdy"), slot + 1)
                pe.wait_ge(S("down_low"), 2 * slot + 2)
                if later(slot):
                    pe.wait_ge(S("yo_rdy"), 2 * slot)
                for half in range(2):
                    split_product(pb[:, 5 + half, :], axH, axL, "down", half * 512, (half + 1) * 512).then_inc(S("down_mm"), 1)

            turn_rows(0)
            gate_up(0)
            turn_product(0)
            turn_rows(1)
            down(0)
            with pe.Fori(1, SLOTS - 1) as slot:
                gate_up(slot)
                turn_product(slot)
                turn_rows(slot + 1)
                down(slot)
            gate_up(SLOTS - 1)
            turn_product(SLOTS - 1)
            down(SLOTS - 1)

        USED = {"gate": 1, "up": 1, "down": 2}

        @block.scalar
        def _(act):
            def split_high(slot, w):
                act.wait_ge(S(w + "_in"), 16 * slot + 16)
                if later(slot):
                    act.wait_ge(S(w + "_mm"), USED[w] * slot)
                for c in range(2):
                    act.copy(part(high[w], c), part(raw[w], c)).then_inc(S(w + "_high"), 1)

            def high_rows(slot):
                act.wait_ge(S("hxT_rdy"), 2 * slot + 2)
                if later(slot):
                    act.wait_ge(S("up_mm"), slot)
                act.copy(hxH[:, :, :], hxT[:, :, :]).then_inc(S("hxH_rdy"), 1)

            def activate(slot):
                act.wait_ge(S("gate_mm"), slot + 1)
                if later(slot):
                    act.wait_ge(S("ax_rdy"), slot)
                act.activation(sg[:, :], pb[:, 2, :], ACT.Silu).then_inc(S("sg_rdy"), 1)

            def high_product(slot):
                act.wait_ge(S("axT_rdy"), slot + 1)
                if later(slot):
                    act.wait_ge(S("down_mm"), 2 * slot)
                act.copy(axH[:, :, :], axT[:, :, :]).then_inc(S("axH_rdy"), 1)

            def copy_down(slot):
                if later(slot):
                    act.wait_ge(S("yo_st"), 16 * slot)
                for half in range(2):
                    act.wait_ge(S("down_mm"), 2 * slot + 1 + half)
                    act.copy(yo[:, half * 512:(half + 1) * 512], pb[:, 5 + half, :]).then_inc(S("yo_rdy"), 1)

            def slot_steps(slot, more):
                activate(slot)
                if more:
                    split_high(slot + 1, "gate")
                high_product(slot)
                if more:
                    high_rows(slot + 1)
                    split_high(slot + 1, "up")
                copy_down(slot)
                if more:
                    split_high(slot + 1, "down")

            high_rows(0)
            for w in SHAPES:
                split_high(0, w)
            slot_steps(0, True)
            with act.Fori(1, SLOTS - 1) as slot:
                slot_steps(slot, True)
            slot_steps(SLOTS - 1, False)

        @block.vector
        def _(dve):
            def index(slot):
                if later(slot):
                    dve.wait_ge(S("hx_in"), 16 * slot)
                dve.tensor_copy(tix[:, :], tokx[:, bass.ds(slot, 1)]).then_inc(S("tix_rdy"), 1)

            def turned_rows(slot):
                if later(slot):
                    dve.wait_ge(S("hxL_rdy"), slot)
                for half in range(2):
                    dve.wait_ge(S("hx_tr"), 2 * slot + 1 + half)
                    dve.tensor_tensor(hxT[:, 4 * half:4 * half + 4, :], pb[:, half, :].rearrange("p (k t) -> p k t", k=4),
                                      bc(cols[:, CO_GFFN + 4 * half:CO_GFFN + 4 * half + 4], 2, [P, 4, P]), ALU.mult).then_inc(S("hxT_rdy"), 1)

            def low_rows(slot):
                dve.wait_ge(S("hxH_rdy"), slot + 1)
                if later(slot):
                    dve.wait_ge(S("up_mm"), slot)
                dve.tensor_tensor(hxL[:, :, :], hxT[:, :, :], hxH[:, :, :].bitcast(F32), ALU.subtract).then_inc(S("hxL_rdy"), 1)

            def split_low(slot, w, c):
                dve.wait_ge(S(w + "_high"), 2 * slot + 1 + c)
                if later(slot):
                    dve.wait_ge(S(w + "_mm"), USED[w] * slot)
                dve.tensor_tensor(part(low_[w], c), part(raw[w], c), part(high[w], c).bitcast(F32), ALU.subtract).then_inc(S(w + "_low"), 1)

            def product(slot):
                dve.wait_ge(S("sg_rdy"), slot + 1)
                dve.wait_ge(S("up_mm"), slot + 1)
                if later(slot):
                    dve.wait_ge(S("ax_tr"), slot)
                dve.tensor_tensor(ax[:, :], pb[:, 3, :], sg[:, :], ALU.mult).then_inc(S("ax_rdy"), 1)

            def turned_product(slot):
                dve.wait_ge(S("ax_tr"), slot + 1)
                if later(slot):
                    dve.wait_ge(S("axL_rdy"), slot)
                dve.tensor_copy(axT[:, :, :], pb[:, 4, :].rearrange("p (k t) -> p k t", k=KF)).then_inc(S("axT_rdy"), 1)

            def low_product(slot):
                dve.wait_ge(S("axH_rdy"), slot + 1)
                if later(slot):
                    dve.wait_ge(S("down_mm"), 2 * slot)
                dve.tensor_tensor(axL[:, :, :], axT[:, :, :], axH[:, :, :].bitcast(F32), ALU.subtract).then_inc(S("axL_rdy"), 1)

            def slot_steps(slot, more):
                if more:
                    split_low(slot + 1, "gate", 0)
                product(slot)
                turned_product(slot)
                low_product(slot)
                if more:
                    turned_rows(slot + 1)
                    if more > 1:
                        index(slot + 2)
                    low_rows(slot + 1)
                    split_low(slot + 1, "gate", 1)
                    split_low(slot + 1, "up", 0)
                    split_low(slot + 1, "up", 1)
                    split_low(slot + 1, "down", 0)
                    split_low(slot + 1, "down", 1)

            index(0)
            turned_rows(0)
            index(1)
            low_rows(0)
            for w in SHAPES:
                split_low(0, w, 0)
                split_low(0, w, 1)
            slot_steps(0, 2)
            with dve.Fori(1, SLOTS - 2) as slot:
                slot_steps(slot, 2)
            slot_steps(SLOTS - 2, 1)
            slot_steps(SLOTS - 1, 0)

        block.__exit__(None, None, None)
        p5.close()
        end_phase()

        p6 = ExitStack()
        wpg = sb_in(p6, "wpg", [P, KD, D])
        wpp = sb_in(p6, "wpp", [P, PLE // P, D])
        x3 = sb_in(p6, "x3", [P, TILES, D])
        pix = sb_in(p6, "pix", [P, 2], U32)
        ye = [sb_in(p6, f"ye{k}", [P, D]) for k in range(2)]
        pT6 = sb_in(p6, "pT6", [P, PLE // P, P])
        xg = sb_in(p6, "xg", [P, D])
        xgT = sb_in(p6, "xgT", [P, KD, P])
        sgm = sb_in(p6, "sgm", [P, D])
        prj = sb_in(p6, "prj", [P, D])
        x4 = sb_in(p6, "x4", [P, D])
        fsq = sb_in(p6, "fsq", [P, D])
        yf = sb_in(p6, "yf", [P, D])
        st6 = sb_in(p6, "st6", [P, 6])

        block = nc.Block()
        block.__enter__()

        @block.sync
        def _(sp):
            for i in range(TILES):
                sp.dma_start(x3[:, i, :], x2_d[i * P:(i + 1) * P, :]).then_inc(S("x3_in") if i else S("x3_first"), 16)
                if i == 0:
                    sp.dma_start(pT6[:, :, :], p_rows[:, 0:P].rearrange("(k p) t -> p k t", p=P)).then_inc(S("pT6_in"), 16)
                    wv = w_pg.rearrange("(k p) n -> p k n", p=P)
                    for half in range(2):
                        sp.dma_start(wpg[:, :, half * 512:(half + 1) * 512], wv[:, :, half * 512:(half + 1) * 512]).then_inc(S(f"wpg_in{half}"), 16)
                    sp.dma_start(wpp[:, :, :], w_pp.rearrange("(k p) n -> p k n", p=P)).then_inc(S("wpp_in"), 16)
            with sp.Fori(1, TILES) as i:
                sp.wait_ge(S("prj_mm"), i * 2)
                sp.dma_start(pT6[:, :, :], p_rows[:, bass.ds(i * P, P)].rearrange("(k p) t -> p k t", p=P)).then_inc(S("pT6_in"), 16)
                sp.wait_ge(S("yf_rdy"), i)
                sp.dma_start(t_out["y"][bass.ds(i * P - P, P), :], yf[:, :]).then_inc(S("y_st"), 16)
            sp.wait_ge(S("yf_rdy"), TILES)
            sp.dma_start(t_out["y"][(TILES - 1) * P:, :], yf[:, :]).then_inc(S("y_st"), 16)
            sp.wait_ge(S("y_st"), 16 * TILES)

        @block.gpsimd
        def _(pool):
            def inverse_root(i, at, name, used):
                pool.wait_ge(S(name + "_sq"), i + 1)
                if later(i):
                    pool.wait_ge(S(used), i)
                pool.tensor_tensor(st6[:, at + 1:at + 2], st6[:, at:at + 1], meps[:, 0:1], ALU.add).then_inc(S(name + "_var"), 1)
                pool.wait_ge(S(name + "_var"), i + 1)
                pool.tensor_tensor(st6[:, at + 2:at + 3], st6[:, at + 1:at + 2], mhalf[:, 0:1], ALU.pow).then_inc(S(name + "_rs"), 1)

            def gather(i):
                pool.wait_ge(S("pix_rdy"), i + 1)
                if later(i):
                    pool.wait_ge(S("x3_rdy"), 2 * i)
                    pool.wait_ge(S("mark6_rdy"), i)
                    pool.tensor_tensor(mark[:, :], meps[:, 0:1], meps[:, 0:1], ALU.add).then_inc(S("mark6_rdy"), 1)
                for k in range(2):
                    pool.indirect_dma_start(out=ye[k][:, :], out_offset=None, in_=y_d[:, :],
                                            in_offset=bass.IndirectOffsetOnAxis(ap=pix[:, k:k + 1], axis=0)).then_inc(S(f"ye{k}_in"), 16)

            pool.memset(mark[:, :], 0.0).then_inc(S("mark6_rdy"), 1)
            gather(0)
            inverse_root(0, 0, "g", "xg_rdy")
            with pool.Fori(1, TILES) as i:
                gather(i)
                inverse_root(i, 0, "g", "xg_rdy")
                inverse_root(i - 1, 3, "f", "yf_rdy")
            inverse_root(TILES - 1, 3, "f", "yf_rdy")

        @block.tensor
        def _(pe):
            def turn_rows(i):
                pe.wait_ge(S("xg_rdy"), i + 1)
                if later(i):
                    pe.wait_ge(S("xgT_rdy"), 2 * i)
                for half in range(2):
                    for k in range(4):
                        last = pe.transpose(pb[:, half, k * P:(k + 1) * P], xg[:, (4 * half + k) * P:(4 * half + k + 1) * P], ident)
                    last.then_inc(S("xg_tr"), 1)

            def gate(i):
                pe.wait_ge(S("xgT_rdy"), 2 * i + 2)
                if not later(i):
                    pe.wait_ge(S("wpg_in0"), 16)
                    pe.wait_ge(S("wpg_in1"), 16)
                if later(i):
                    pe.wait_ge(S("sgm_rdy"), 2 * i)
                for half in range(2):
                    for k in range(KD):
                        last = pe.matmul(pb[:, 2 + half, :], xgT[:, k, :], wpg[:, k, half * 512:(half + 1) * 512], start=k == 0, stop=k == KD - 1)
                    last.then_inc(S("open_mm"), 1)

            def embed(i):
                pe.wait_ge(S("pT6_in"), 16 * i + 16)
                if not later(i):
                    pe.wait_ge(S("wpp_in"), 16)
                if later(i):
                    pe.wait_ge(S("prj_rdy"), 2 * i)
                for half in range(2):
                    for k in range(PLE // P):
                        last = pe.matmul(pb[:, 4 + half, :], pT6[:, k, :], wpp[:, k, half * 512:(half + 1) * 512], start=k == 0, stop=k == PLE // P - 1)
                    last.then_inc(S("prj_mm"), 1)

            turn_rows(0)
            gate(0)
            turn_rows(1)
            embed(0)
            with pe.Fori(1, TILES - 1) as i:
                gate(i)
                turn_rows(i + 1)
                embed(i)
            gate(TILES - 1)
            embed(TILES - 1)

        @block.scalar
        def _(act):
            def norm_rows(i):
                act.wait_ge(S("x3_rdy"), 2 * i + 2)
                if later(i):
                    act.wait_ge(S("g_rs"), i)
                    act.wait_ge(S("xg_tr"), 2 * i)
                act.activation(xg[:, :], x3[:, bass.ds(i, 1), :].rearrange("p a n -> p (a n)"), ACT.Square, scale=D ** -0.5, accum_out=st6[:, 0:1]).then_inc(S("g_sq"), 1)
                act.wait_ge(S("g_rs"), i + 1)
                if later(i):
                    act.wait_ge(S("act_mark6"), i)
                act.activation(amark[:, :], meps[:, 0:1], ACT.Copy).then_inc(S("act_mark6"), 1)
                act.activation(xg[:, :], x3[:, bass.ds(i, 1), :].rearrange("p a n -> p (a n)"), ACT.Copy, scale=st6[:, 2:3]).then_inc(S("xg_rdy"), 1)

            def open_gate(i):
                if later(i):
                    act.wait_ge(S("prj_rdy"), 2 * i)
                for half in range(2):
                    act.wait_ge(S("open_mm"), 2 * i + 1 + half)
                    act.activation(sgm[:, half * 512:(half + 1) * 512], pb[:, 2 + half, :], ACT.Sigmoid).then_inc(S("sgm_rdy"), 1)

            def last_norm(i):
                act.wait_ge(S("x4_rdy"), i + 1)
                if later(i):
                    act.wait_ge(S("f_rs"), i)
                    act.wait_ge(S("f_sq"), i)
                act.activation(fsq[:, :], x4[:, :], ACT.Square, scale=D ** -0.5, accum_out=st6[:, 3:4]).then_inc(S("f_sq"), 1)

            norm_rows(0)
            with act.Fori(0, TILES - 1) as i:
                norm_rows(i + 1)
                open_gate(i)
                last_norm(i)
            open_gate(TILES - 1)
            last_norm(TILES - 1)

        @block.vector
        def _(dve):
            def index(i):
                if later(i):
                    dve.wait_ge(S("ye0_in"), 16 * i)
                    dve.wait_ge(S("ye1_in"), 16 * i)
                dve.tensor_copy(pix[:, :], posg[:, :, bass.ds(i, 1)].rearrange("p k a -> p (k a)")).then_inc(S("pix_rdy"), 1)

            def experts_sum(i):
                x = x3[:, bass.ds(i, 1), :].rearrange("p a n -> p (a n)")
                if later(i):
                    dve.wait_ge(S("x3_in"), 16 * (TILES - 1))
                else:
                    dve.wait_ge(S("x3_first"), 16)
                for k in range(2):
                    dve.wait_ge(S(f"ye{k}_in"), 16 * i + 16)
                    if k:
                        dve.wait_ge(S("x3_rdy"), 2 * i + 1)
                    dve.scalar_tensor_tensor(x, ye[k][:, :], gates[:, k, bass.ds(i, 1)], x, ALU.mult, ALU.add).then_inc(S("x3_rdy"), 1)

            def turned_rows(i):
                for half in range(2):
                    dve.wait_ge(S("xg_tr"), 2 * i + 1 + half)
                    if half == 0 and later(i):
                        dve.wait_ge(S("open_mm"), 2 * i)
                    dve.tensor_tensor(xgT[:, 4 * half:4 * half + 4, :], pb[:, half, :].rearrange("p (k t) -> p k t", k=4),
                                      bc(cols[:, CO_GPLE + 4 * half:CO_GPLE + 4 * half + 4], 2, [P, 4, P]), ALU.mult).then_inc(S("xgT_rdy"), 1)

            def gated(i):
                if later(i):
                    dve.wait_ge(S("x4_rdy"), i)
                for half in range(2):
                    a = slice(half * 512, (half + 1) * 512)
                    dve.wait_ge(S("sgm_rdy"), 2 * i + 1 + half)
                    dve.wait_ge(S("prj_mm"), 2 * i + 1 + half)
                    dve.tensor_tensor(prj[:, a], pb[:, 4 + half, :], sgm[:, a], ALU.mult).then_inc(S("prj_rdy"), 1)
                dve.wait_ge(S("prj_rdy"), 2 * i + 2)
                if later(i):
                    dve.wait_ge(S("yf_rdy"), i)
                dve.tensor_tensor(x4[:, :], prj[:, :], x3[:, bass.ds(i, 1), :].rearrange("p a n -> p (a n)"), ALU.add).then_inc(S("x4_rdy"), 1)

            def output(i):
                dve.wait_ge(S("f_rs"), i + 1)
                if later(i):
                    dve.wait_ge(S("y_st"), 16 * i)
                dve.scalar_tensor_tensor(yf[:, :], x4[:, :], st6[:, 5:6], brow[:, BR_GFIN:BR_GFIN + D], ALU.mult, ALU.mult).then_inc(S("yf_rdy"), 1)

            index(0)
            experts_sum(0)
            turned_rows(0)
            index(1)
            experts_sum(1)
            turned_rows(1)
            gated(0)
            with dve.Fori(1, TILES - 1) as i:
                index(i + 1)
                experts_sum(i + 1)
                turned_rows(i + 1)
                output(i - 1)
                gated(i)
            output(TILES - 2)
            gated(TILES - 1)
            output(TILES - 1)

        block.__exit__(None, None, None)
        p6.close()
        end_phase()



def rope_rows():
    half = ROPE // 2
    inv = np.float32(10000.0) ** (-np.arange(half, dtype=np.float32) / half)
    pos = np.concatenate([np.arange(SEQ), np.full(P, PAGES * P)]).astype(np.float32)
    ang = pos[:, None] * inv[None, :]
    return np.concatenate([np.cos(ang), np.sin(ang)], 1).astype(np.float32)


def shape_constants():
    c = np.zeros((P, CS_W), np.float32)
    i = np.arange(P)
    c[:, CS_ID:CS_ID + P] = np.eye(P)
    c[:, CS_TRI:CS_TRI + P] = i[:, None] <= i[None, :]
    c[:, CS_CAUS:CS_CAUS + P] = np.where(i[None, :] <= i[:, None], 0.0, NEG)
    c[:, CS_NEW:CS_NEW + NB] = np.where(i[:, None] == np.arange(NB)[None, :], 0.0, NEG)
    c[:, CS_EYE:CS_EYE + NB * NB] = np.eye(NB).reshape(1, -1)
    c[:, CS_HSEL:CS_HSEL + H] = i[:, None] % H == np.arange(H)[None, :]
    c[:, CS_SEL32:CS_SEL32 + H] = i[:, None] % 32 == np.arange(H)[None, :]
    c[:, CS_NEG:CS_NEG + 255] = np.where(np.arange(255) == 127, 0.0, NEG)[None, :]
    c[:, CS_IOTA:CS_IOTA + P] = i[None, :]
    c[:, CS_REV:CS_REV + NE] = NE - np.arange(NE)[None, :]
    c[:, CS_LOW:CS_LOW + NE * NE] = np.tril(np.ones((NE, NE)), -1).reshape(1, -1)
    c[:, CS_VALID] = i < NB
    c[:, CS_TOK:CS_TOK + TILES] = np.arange(TILES)[None, :] * P + i[:, None]
    return c


def layouts(x):
    f = {k: np.asarray(v) for k, v in x.items()}
    col = lambda v: v.reshape(-1, P).T
    pad = np.zeros((2 * P - NB, D), np.float32)
    row = np.concatenate([f["norm_kv"][0], f["norm_final"], f["dt_bias"][0], f["a_log"][0], f["d_skip"][0],
                          f["b_group_router"][0], f["b_expert_router"][0]])
    return {
        "x_all": np.concatenate([f["x_prompt"][0], f["x_sample"][:, 0], pad]),
        "p_t": np.concatenate([f["p_prompt"][0, 0], f["p_sample"][0, :, 0], pad[:P - NB, :PLE]]).T,
        "cache": np.concatenate([f["cache_ckv"][0], f["cache_krope"][0]], -1),
        "page_table": f["page_table"].reshape(NB, 8, 4).transpose(0, 2, 1).reshape(1, -1),
        "conv_prev": f["state_conv"][0].transpose(2, 1, 0).reshape(CT, P, CK - 1, NB).transpose(1, 0, 2, 3),
        "ssm_prev": f["state_ssm"][0].transpose(3, 0, 1, 2).reshape(P, -1),
        "brow": np.broadcast_to(row, (P, BR_W)),
        "cols": np.concatenate([col(f["norm_mix"][0]), col(f["norm_q"][0]), col(f["norm_attn_out"][0]), col(f["norm_ssm_out"][0]),
                                col(f["norm_ffn"][0]), col(f["norm_ple"][0]),
                                f["conv_w"][0].reshape(CK, CT, P).transpose(2, 1, 0).reshape(P, -1), col(f["conv_b"][0])], 1),
        "cst": shape_constants(),
        "rope": rope_rows(),
        "w_in": f["w_in"][0],
        "w_uq": f["w_uq"][0].reshape(QL, -1),
        "w_ukv": f["w_ukv"][0].reshape(KL, -1),
        "w_ukt": f["w_ukv"][0][:, :, :NOPE].transpose(2, 1, 0),
        "w_out": f["w_out"][0],
        "w_rout": np.concatenate([f["w_group_router"][0], f["w_expert_router"][0]], 1),
        "w_gate": f["w_exp_gate"][0].reshape(NE * D, FF),
        "w_up": f["w_exp_up"][0].reshape(NE * D, FF),
        "w_down": f["w_exp_down"][0].reshape(NE * FF, D),
        "w_pg": f["w_ple_gate"][0],
        "w_pp": f["w_ple_proj"][0],
    }


OUTS = {"y": (ROWS, D), "ckv": (ROWS, KL), "krope": (ROWS, ROPE), "conv_p": (P, CT, CK - 1), "ssm_p": (P, INNER),
        "conv_s": (P, CT, CK - 1, NB), "ssm_s": (P, NB * INNER)}


def results(y, ckv, krope, conv_p, ssm_p, conv_s, ssm_s):
    return (y[:SEQ][None], y[SEQ:SEQ + NB][:, None],
            ckv[:SEQ][None, None], krope[:SEQ][None, None],
            conv_p.transpose(2, 1, 0).reshape(1, 1, CK - 1, CT * P), ssm_p.reshape(NST, H, 64).transpose(1, 2, 0)[None, None],
            ckv[SEQ:SEQ + NB][None, :, None], krope[SEQ:SEQ + NB][None, :, None],
            conv_s.transpose(3, 2, 1, 0).reshape(1, NB, CK - 1, CT * P), ssm_s.reshape(NST, NB, H, 64).transpose(1, 2, 3, 0)[None])


def kernel(**inputs):
    import concourse.bacc as _bacc
    from concourse.bass_utils import run_bass_kernel_spmd as _run

    nc = _bacc.Bacc("TRN2", target_bir_lowering=False, num_devices=1)
    arrays = {"in_" + name: np.ascontiguousarray(a) for name, a in layouts(inputs).items()}
    t_in = {name[3:]: nc.dram_tensor(name, a.shape, mybir.dt.from_np(a.dtype), kind="ExternalInput").ap() for name, a in arrays.items()}
    t_out = {name: nc.dram_tensor("out_" + name, shape, F32, kind="ExternalOutput").ap() for name, shape in OUTS.items()}
    program(nc, t_in, t_out)
    r = _run(nc, [arrays], core_ids=[0])
    return results(*[r.results[0]["out_" + name] for name in OUTS])
```
